# Optimizing a Trainium2 kernel written in Bass

```python
import jax, jax.numpy as jnp
from jax import lax
import numpy as np

D_MODEL = 1024
BATCH = 1
SEQ = 256
DEPTH = 1
DEC_BATCH = 8
DEC_SEQ = 8
PAST_LEN = 2048
PAGE_SIZE = 128

W_LRU = D_MODEL
N_LRU_BLOCKS = 8
LRU_BLOCK = W_LRU // N_LRU_BLOCKS
CONV_WIDTH = 4
LRU_C = 8.0
RWKV_HEAD = 64
N_RWKV_HEADS = D_MODEL // RWKV_HEAD
W_RWKV = N_RWKV_HEADS * RWKV_HEAD
LORA_W = 64
LORA_A = 64
LORA_G = 160
RWKV_COLS = 3 * W_RWKV + LORA_W + LORA_A + LORA_G
GN_EPS = 64e-5
IN_COLS = 2 * W_LRU + RWKV_COLS + 2 * D_MODEL
N_GROUPS = 4
EXPERTS_PER_GROUP = 8
N_EXPERTS = N_GROUPS * EXPERTS_PER_GROUP
D_EXPERT = 256
TOP_K_INNER = 2
NORM_EPS = 1e-6

kernel_name = 'hawk_rwkv7_hier_moe_step'

def _rmsnorm(x, gain):
    xf = x.astype(jnp.float32)
    return xf * lax.rsqrt(jnp.mean(xf * xf, axis=-1, keepdims=True) + NORM_EPS) * gain

def _causal_conv(xa, buf, w, b):
    T = xa.shape[1]
    xp = jnp.concatenate([buf.astype(jnp.float32), xa.astype(jnp.float32)], axis=1)
    out = b + sum(w[j] * xp[:, j:j + T] for j in range(CONV_WIDTH))
    return out, xp[:, T:]

def _lin_combine(left, right):
    a_l, b_l = left
    a_r, b_r = right
    return a_l * a_r, a_r * b_l + b_r

def _rglru(x, h0, wx, bx, wa, ba, a_param, reset_first):
    B, T, _ = x.shape
    x = x.astype(jnp.float32)
    xb = x.reshape(B, T, N_LRU_BLOCKS, LRU_BLOCK)
    gate_x = jax.nn.sigmoid(jnp.einsum('btnd,nde->btne', xb, wx).reshape(B, T, W_LRU) + bx)
    gate_a = jax.nn.sigmoid(jnp.einsum('btnd,nde->btne', xb, wa).reshape(B, T, W_LRU) + ba)
    log_a = LRU_C * gate_a * jax.nn.log_sigmoid(a_param)
    a = jnp.exp(log_a)
    mult = jnp.sqrt(-jnp.expm1(2.0 * log_a))
    if reset_first:
        mult = mult.at[:, 0].set(1.0)
    bterm = x * gate_x * mult
    a_cum, b_cum = lax.associative_scan(_lin_combine, (a, bterm), axis=1)
    h = b_cum + a_cum * h0.astype(jnp.float32)[:, None]
    return h, h[:, -1]

def _wkv_scan(r, decay, k, v, aa, bb, S0):
    def step(S, inp):
        r_t, w_t, k_t, v_t, a_t, b_t = inp
        Sa = jnp.einsum('bhij,bhj->bhi', S, a_t)
        S = S * w_t[:, :, None, :] + Sa[..., None] * b_t[:, :, None, :] + v_t[..., None] * k_t[:, :, None, :]
        y = jnp.einsum('bhij,bhj->bhi', S, r_t)
        return S, y
    xs = tuple(jnp.moveaxis(z, 1, 0) for z in (r, decay, k, v, aa, bb))
    S, ys = lax.scan(step, S0, xs)
    return jnp.moveaxis(ys, 0, 1), S

def _rwkv7(P, prev, S0, mu, w0, w2, a0, a2, g2, k_k, k_a, r_k, ln_w, ln_b):
    B, T, _ = P.shape
    P = P.astype(jnp.float32)
    P_prev = jnp.concatenate([prev.astype(jnp.float32)[:, None], P[:, :-1]], axis=1)
    Pm = P + (P_prev - P) * mu
    c1, c2, c3 = W_RWKV, 2 * W_RWKV, 3 * W_RWKV
    r, k, v, xw, xa, xg = jnp.split(Pm, [c1, c2, c3, c3 + LORA_W, c3 + LORA_W + LORA_A], axis=-1)
    w_log = -jax.nn.softplus(-(w0 + jnp.tanh(xw) @ w2)) - 0.5
    decay = jnp.exp(-jnp.exp(w_log))
    a = jax.nn.sigmoid(a0 + xa @ a2)
    g = jax.nn.sigmoid(xg) @ g2
    hs = (B, T, N_RWKV_HEADS, RWKV_HEAD)
    kk = (k * k_k).reshape(hs)
    kk = kk / jnp.maximum(jnp.sqrt(jnp.sum(kk * kk, axis=-1, keepdims=True)), 1e-12)
    k = k * (1.0 + (a - 1.0) * k_a)
    rh, kh, vh, ah = r.reshape(hs), k.reshape(hs), v.reshape(hs), a.reshape(hs)
    y, S = _wkv_scan(rh, decay.reshape(hs), kh, vh, -kk, kk * ah, S0.astype(jnp.float32))
    mean = jnp.mean(y, axis=-1, keepdims=True)
    var = jnp.mean(jnp.square(y - mean), axis=-1, keepdims=True)
    yn = ((y - mean) * lax.rsqrt(var + GN_EPS)).reshape(B, T, W_RWKV) * ln_w + ln_b
    bonus = jnp.sum(rh * kh * r_k, axis=-1, keepdims=True) * vh
    out = (yn + bonus.reshape(B, T, W_RWKV)) * g
    return out, P[:, -1], S

def _hier_moe(x, rg, rgb, re, reb, wg, wu, wd):
    B, T, D = x.shape
    t = x.reshape(B * T, D)
    pg = jax.nn.softmax((t @ rg + rgb).astype(jnp.float32), axis=-1)
    p_top, g_idx = lax.top_k(pg, 1)
    le = (t @ re + reb).astype(jnp.float32).reshape(-1, N_GROUPS, EXPERTS_PER_GROUP)
    le_g = jnp.take_along_axis(le, g_idx[:, :, None], axis=1)[:, 0]
    q, e_idx = lax.top_k(jax.nn.softmax(le_g, axis=-1), TOP_K_INNER)
    q = q / jnp.sum(q, axis=-1, keepdims=True)
    w_grp = jnp.sum(jax.nn.one_hot(e_idx, EXPERTS_PER_GROUP) * q[..., None], axis=1)
    comb = (jax.nn.one_hot(g_idx[:, 0], N_GROUPS)[:, :, None] * w_grp[:, None, :] * p_top[:, :, None]).reshape(-1, N_EXPERTS)
    h = jax.nn.silu(jnp.einsum('nd,edf->nef', t, wg)) * jnp.einsum('nd,edf->nef', t, wu)
    h = h * comb[:, :, None]
    y = jnp.einsum('nef,efd->nd', h, wd)
    return y.reshape(B, T, D)

def _layer(x, conv_buf, h0, shift_prev, wkv0, reset_first, norm1, w_in, conv_w, conv_b, lru_wx, lru_bx, lru_wa, lru_ba, lru_a_param, rwkv_mu, rwkv_w0, rwkv_w2, rwkv_a0, rwkv_a2, rwkv_g2, rwkv_k_k, rwkv_k_a, rwkv_r_k, rwkv_ln_w, rwkv_ln_b, w_out, norm2, router_group, router_group_b, router_expert, router_expert_b, exp_gate, exp_up, exp_down):
    xn = _rmsnorm(x, norm1)
    proj = xn @ w_in
    s1 = W_LRU
    s2 = 2 * W_LRU
    s3 = s2 + RWKV_COLS
    s4 = s3 + D_MODEL
    lru_x, lru_y, rw, gate_lru, gate_rwkv = jnp.split(proj, [s1, s2, s3, s4], axis=-1)
    xc, new_conv = _causal_conv(lru_x, conv_buf, conv_w, conv_b)
    h, h_last = _rglru(xc, h0, lru_wx, lru_bx, lru_wa, lru_ba, lru_a_param, reset_first)
    out_lru = h * jax.nn.gelu(lru_y)
    out_rwkv, new_shift, new_wkv = _rwkv7(rw, shift_prev, wkv0, rwkv_mu, rwkv_w0, rwkv_w2, rwkv_a0, rwkv_a2, rwkv_g2, rwkv_k_k, rwkv_k_a, rwkv_r_k, rwkv_ln_w, rwkv_ln_b)
    merged = jax.nn.sigmoid(gate_lru) * out_lru + jax.nn.sigmoid(gate_rwkv) * out_rwkv
    x = x + merged @ w_out
    x = x + _hier_moe(_rmsnorm(x, norm2), router_group, router_group_b, router_expert, router_expert_b, exp_gate, exp_up, exp_down)
    return x, new_conv, h_last, new_shift, new_wkv

def setup_inputs(seed: int = 0) -> dict:
    key = jax.random.key(seed)
    ks = iter(jax.random.split(key, 64))
    f32 = jnp.float32

    def nrm(shape, scale):
        return scale * jax.random.normal(next(ks), shape, f32)

    def uni(shape, lo, hi):
        return jax.random.uniform(next(ks), shape, f32, lo, hi)

    L = DEPTH
    a_lru = uni((L, W_LRU), 0.9, 0.999) ** (1.0 / LRU_C)
    return {
        'x_prompt': nrm((BATCH, SEQ, D_MODEL), 1.0),
        'x_sample': nrm((DEC_BATCH, DEC_SEQ, D_MODEL), 1.0),
        'state_conv': nrm((L, DEC_BATCH, CONV_WIDTH - 1, W_LRU), 1.0),
        'state_lru': nrm((L, DEC_BATCH, W_LRU), 0.5),
        'state_shift': nrm((L, DEC_BATCH, RWKV_COLS), 1.0),
        'state_wkv': nrm((L, DEC_BATCH, N_RWKV_HEADS, RWKV_HEAD, RWKV_HEAD), 0.3),
        'norm1': 1.0 + nrm((L, D_MODEL), 0.05),
        'w_in': nrm((L, D_MODEL, IN_COLS), D_MODEL ** -0.5),
        'conv_w': nrm((L, CONV_WIDTH, W_LRU), CONV_WIDTH ** -0.5),
        'conv_b': nrm((L, W_LRU), 0.02),
        'lru_wx': nrm((L, N_LRU_BLOCKS, LRU_BLOCK, LRU_BLOCK), LRU_BLOCK ** -0.5),
        'lru_bx': nrm((L, W_LRU), 0.02),
        'lru_wa': nrm((L, N_LRU_BLOCKS, LRU_BLOCK, LRU_BLOCK), LRU_BLOCK ** -0.5),
        'lru_ba': nrm((L, W_LRU), 0.02),
        'lru_a_param': jnp.log(a_lru) - jnp.log1p(-a_lru),
        'rwkv_mu': uni((L, RWKV_COLS), 0.0, 1.0),
        'rwkv_w0': uni((L, W_RWKV), -6.0, 1.0),
        'rwkv_w2': nrm((L, LORA_W, W_RWKV), 0.5 * LORA_W ** -0.5),
        'rwkv_a0': nrm((L, W_RWKV), 0.1),
        'rwkv_a2': nrm((L, LORA_A, W_RWKV), 0.5 * LORA_A ** -0.5),
        'rwkv_g2': nrm((L, LORA_G, W_RWKV), LORA_G ** -0.5),
        'rwkv_k_k': 0.85 + nrm((L, W_RWKV), 0.05),
        'rwkv_k_a': 1.0 + nrm((L, W_RWKV), 0.05),
        'rwkv_r_k': nrm((L, N_RWKV_HEADS, RWKV_HEAD), 0.1),
        'rwkv_ln_w': 1.0 + nrm((L, W_RWKV), 0.05),
        'rwkv_ln_b': nrm((L, W_RWKV), 0.02),
        'w_out': nrm((L, D_MODEL, D_MODEL), D_MODEL ** -0.5),
        'norm2': 1.0 + nrm((L, D_MODEL), 0.05),
        'router_group': nrm((L, D_MODEL, N_GROUPS), D_MODEL ** -0.5),
        'router_group_b': nrm((L, N_GROUPS), 0.01),
        'router_expert': nrm((L, D_MODEL, N_EXPERTS), D_MODEL ** -0.5),
        'router_expert_b': nrm((L, N_EXPERTS), 0.01),
        'exp_gate': nrm((L, N_EXPERTS, D_MODEL, D_EXPERT), D_MODEL ** -0.5),
        'exp_up': nrm((L, N_EXPERTS, D_MODEL, D_EXPERT), D_MODEL ** -0.5),
        'exp_down': nrm((L, N_EXPERTS, D_EXPERT, D_MODEL), D_EXPERT ** -0.5),
        'final_norm': 1.0 + nrm((D_MODEL,), 0.05),
    }

def reference(x_prompt, x_sample, state_conv, state_lru, state_shift, state_wkv, norm1, w_in, conv_w, conv_b, lru_wx, lru_bx, lru_wa, lru_ba, lru_a_param, rwkv_mu, rwkv_w0, rwkv_w2, rwkv_a0, rwkv_a2, rwkv_g2, rwkv_k_k, rwkv_k_a, rwkv_r_k, rwkv_ln_w, rwkv_ln_b, w_out, norm2, router_group, router_group_b, router_expert, router_expert_b, exp_gate, exp_up, exp_down, final_norm):
    f32 = jnp.float32
    hp = x_prompt
    hs = x_sample
    conv_p, lru_p, shift_p, wkv_p = [], [], [], []
    conv_s, lru_s, shift_s, wkv_s = [], [], [], []
    for l in range(DEPTH):
        lp = (norm1[l], w_in[l], conv_w[l], conv_b[l], lru_wx[l], lru_bx[l], lru_wa[l], lru_ba[l], lru_a_param[l], rwkv_mu[l], rwkv_w0[l], rwkv_w2[l], rwkv_a0[l], rwkv_a2[l], rwkv_g2[l], rwkv_k_k[l], rwkv_k_a[l], rwkv_r_k[l], rwkv_ln_w[l], rwkv_ln_b[l], w_out[l], norm2[l], router_group[l], router_group_b[l], router_expert[l], router_expert_b[l], exp_gate[l], exp_up[l], exp_down[l])
        hp, c, h, s, w = _layer(hp, jnp.zeros((BATCH, CONV_WIDTH - 1, W_LRU), f32), jnp.zeros((BATCH, W_LRU), f32), jnp.zeros((BATCH, RWKV_COLS), f32), jnp.zeros((BATCH, N_RWKV_HEADS, RWKV_HEAD, RWKV_HEAD), f32), True, *lp)
        conv_p.append(c)
        lru_p.append(h)
        shift_p.append(s)
        wkv_p.append(w)
        hs, c, h, s, w = _layer(hs, state_conv[l], state_lru[l], state_shift[l], state_wkv[l], False, *lp)
        conv_s.append(c)
        lru_s.append(h)
        shift_s.append(s)
        wkv_s.append(w)
    y_prompt = _rmsnorm(hp, final_norm)
    y_sample = _rmsnorm(hs, final_norm)
    return (y_prompt, y_sample, jnp.stack(conv_p), jnp.stack(lru_p), jnp.stack(shift_p), jnp.stack(wkv_p), jnp.stack(conv_s), jnp.stack(lru_s), jnp.stack(shift_s), jnp.stack(wkv_s))


_drawn_inputs = setup_inputs


def setup_inputs(seed=0):
    import zlib

    import numpy as np

    out = dict(_drawn_inputs(seed))
    spreads = {}
    factors = {'lru_bx': 8.0,
     'lru_ba': 8.0,
     'router_group_b': 4.088,
     'router_expert_b': 3.698,
     'rwkv_ln_b': 5.541}
    for name, (base, spread) in spreads.items():
        noise = np.random.default_rng([zlib.crc32(name.encode()), seed]).standard_normal(out[name].shape)
        drawn = base * np.exp(spread * noise) if base else spread * noise
        out[name] = __import__('jax').numpy.asarray(drawn.astype(out[name].dtype))
    for name, factor in factors.items():
        out[name] = (out[name] * factor).astype(out[name].dtype)
    return out
```

```python
from contextlib import ExitStack

import concourse.bass as bass
from concourse import mybir

F32 = mybir.dt.float32
I32 = mybir.dt.int32
U32 = mybir.dt.uint32
ALU = mybir.AluOpType
ACT = mybir.ActivationFunctionType
AX = mybir.AxisListType

P = 128
D = 1024
KC = D // P
NPROMPT = 256
NB, TB = 8, 8
NSAMPLE = NB * TB
N = NPROMPT + NSAMPLE
TILES = [(0, 128), (128, 128), (256, 64)]
HEAD = 64
PAIRS = 8
CH = 32
NCH = NPROMPT // CH
RWKV = 3 * D + 64 + 64 + 160
NMU = 27
GN_EPS = 64e-5
EPS = 1e-6
E_M05 = 0.6065306597126334
NG, NE_G, NE, DE = 4, 8, 32, 256
CAP = 64
NOV = (2 * N) // (CAP + 1)
ROWS = (NE + NOV) * CAP

COL = {"lx": 0, "ly": D, "r": 2 * D, "k": 3 * D, "v": 4 * D, "gl": 2 * D + RWKV, "gr": 3 * D + RWKV}
TP = [("r", "a"), ("k", "a"), ("v", "a"), ("zw", "a"), ("za", "a"), ("lx", "a"), ("ss", "d"), ("bon", "d"),
      ("ly", "a"), ("gl", "a"), ("gx", "a"), ("ga", "a"), ("gr", "a"), ("g", "d"), ("mean", "d"), ("var", "a")]
TPN = {n: j for j, (n, _) in enumerate(TP)}
NTP = len(TP)
NTPA = sum(e == "a" for _, e in TP)
NTPD = NTP - NTPA

VEC = {"conv_w": 0, "conv_b": 32, "lru_bx": 40, "lru_ba": 48, "a_param": 56, "w0": 64, "a0": 72,
       "k_k": 80, "k_a": 88, "r_k": 96, "ln_w": 104, "ln_b": 112, "norm1": 120}

CONST = {}
_at = 0
for _n, _w in (("ident", 128), ("blk", 128), ("blkmean", 128), ("maskp", 512), ("masks", 256), ("lev", 5 * 128),
               ("m0", N), ("m1", N), ("tri", 128), ("ones", 128), ("bm", 8), ("cm", 4), ("e64", 32), ("g4", 4), ("g8", 8),
               ("j9", NOV), ("misc", 4)):
    CONST[_n] = (_at, _at + _w)
    _at += _w
NCONST = _at


def make_consts():
    import numpy as np
    c = np.zeros((P, NCONST), np.float32)
    r = np.arange(P)[:, None]
    q = np.arange(P)[None, :]

    def put(name, a):
        c[:a.shape[0], CONST[name][0]:CONST[name][0] + a.shape[1]] = a

    put("ident", (r == q) * 1.0)
    put("blk", (r // HEAD == q // HEAD) * 1.0)
    put("blkmean", (r // HEAD == q // HEAD) / HEAD)
    same = r // CH == q // CH
    strict, incl = same & (r < q), same & (r <= q)
    put("maskp", np.concatenate([strict, incl, strict, incl], 1) * 1.0)
    r6, q6 = r[:64], q[:, :64]
    same6 = r6 // TB == q6 // TB
    put("masks", np.concatenate([same6 & (r6 < q6), same6 & (r6 <= q6)] * 2, 1) * 1.0)
    lev = []
    for k in range(5):
        m = 1 << k
        lev.append((r // (2 * m) == q // (2 * m)) & (r // m % 2 == 0) & (q // m % 2 == 1))
    put("lev", np.concatenate(lev, 1) * 1.0)
    t = np.arange(N)
    start = np.where(t < NPROMPT, t % CH == 0, t % TB == 0)
    put("m0", np.tile(1.0 - start, (P, 1)))
    put("m1", np.tile(start * 1.0, (P, 1)))
    put("tri", (r < q) * 1.0)
    put("ones", np.ones((P, P)))
    put("bm", (np.arange(64)[:, None] // TB == np.arange(8)[None]) * 1.0)
    put("cm", (r // CH == np.arange(4)[None]) * 1.0)
    put("e64", np.tile(np.arange(NE) * CAP, (P, 1)))
    put("g4", np.tile(NG - np.arange(NG), (P, 1)))
    put("g8", np.tile(NE_G - np.arange(NE_G), (P, 1)))
    put("j9", np.tile(np.arange(NOV), (P, 1)))
    put("misc", np.tile([[-0.5 * E_M05, GN_EPS, EPS, 1.0]], (P, 1)))
    ids = (np.arange(P)[:, None] + P * np.arange(3)[None]).astype(np.float32)
    return c, ids


class Chain:

    def __init__(self, eng, sem, i=0, per=0):
        self.eng, self.sem, self.base, self.n = eng, sem, (i * per if per else 0), 0

    def go(self, ins):
        ins.then_inc(self.sem, 1)
        self.n += 1

    def wait(self):
        self.eng.wait_ge(self.sem, self.base + self.n)

    def step(self, ins):
        self.go(ins)
        self.wait()


DVE_PER = 78


def hawk_rwkv7_moe(nc, a, o):
    ctx = ExitStack()
    with ctx:
        def sb(name, shape, dt=F32):
            return ctx.enter_context(nc.sbuf_tensor(name, shape, dt))

        sems = {}

        def S(name):
            if name not in sems:
                sems[name] = ctx.enter_context(nc.semaphore("s_" + name))
            return sems[name]

        bank = [ctx.enter_context(nc.psum_tensor(f"bank{j}", [P, 512], F32)) for j in range(8)]

        consts = sb("consts_sb", [P, NCONST])

        def C(name):
            return consts[:, CONST[name][0]:CONST[name][1]]

        ident, blk = C("ident"), C("blk")
        lev = C("lev").rearrange("p (k t) -> p k t", k=5)
        misc = C("misc")
        vrows = sb("vrows", [P, P])
        murows = sb("murows", [NMU, P])
        vT = sb("vT", [P, P])
        muT = sb("muT", [P, NMU])
        half = sb("half", [P, 32])
        ls4 = sb("ls4", [P, 8])
        lst = sb("lst", [P, 3, 8])
        cvT = sb("cvT", [P, KC, 32])
        shT = sb("shT", [P, NMU, NB])
        w2a2 = sb("w2a2", [P, P])
        g2a, g2b = sb("g2a", [P, P]), sb("g2b", [32, P])
        wxa = sb("wxa", [P, 2, P])
        scratch2 = sb("scratch2", [P, 3 * D])
        xt = scratch2[:, :].rearrange("p (t d) -> p t d", t=3)
        scratch = sb("scratch", [P, 4096])
        xn = scratch[:, 0:3 * D].rearrange("p (t d) -> p t d", t=3)
        strows = scratch[0:32, 3 * D:4 * D]
        scratch3 = sb("scratch3", [P, 4096])
        shrows, rowP = scratch3[0:NB, 0:RWKV], scratch3[0:9, 0:NMU * P]
        xnT = sb("xnT", [P, KC, N])
        rowL = xnT[:].rearrange("p k n -> p (k n)")[0:36, 0:D]
        merged = sb("merged", [P, KC, N])
        wall = sb("wall", [P, len(COL) * KC * P])
        wbuf = {n: wall[:, j * KC * P:(j + 1) * KC * P].rearrange("p (k c) -> p k c", k=KC) for j, n in enumerate(COL)}
        wkv = sb("wkv", [P, 6848])
        at = [0]

        def part(*shape):
            n = 1
            for x in shape:
                n *= x
            v = wkv[:, at[0]:at[0] + n]
            at[0] += n
            names = "abcd"[:len(shape)]
            return v.rearrange(f"p ({' '.join(names)}) -> p {' '.join(names)}", **dict(zip(names, shape))) if len(shape) > 1 else v

        lw = part(3, N)
        pad1 = {n: sb("pad1_" + n, [P, 329]) for n in "rkv"}
        pad3 = sb("pad3", [P, 355])
        cacc = sb("cacc", [P, 347])
        lastP = sb("lastP", [P, NMU, 9])
        lastL = sb("lastL", [P, KC, 36])
        dif = sb("dif", [P, 328])
        vecs = sb("vecs", [P, 30 * N])
        (rm, km, vm, kk, kk2, nrm, tw, dec, ta, wsh, ex, Dc, rD, bt, kt, kp, rkk, bon, ysb, ysq, tgl, tgr, xc, tgx, tga,
         la, lth, lm, tu, yT) = (
            vecs[:, j * N:j * N + N] for j, n in enumerate(("rm km vm kk kk2 nrm tw dec ta wsh ex Dc rD bt kt kp rkk bon ysb ysq tgl tgr xc tgx "
                                    "tga la lth lm tu yT").split()))
        hbuf, lruo, yc, yc2, gns, gg = tga, rkk, kp, yT, nrm, kk2
        ar = part(2, N)
        fix = sb("fix", [P, NB])
        am = scratch[:, 0:2048].rearrange("p (u c) -> p u c", u=4)
        ams = sb("ams", [64, 2, 256])
        ak = scratch[:, 2048:4096].rearrange("p (k u c) -> p k u c", k=4, u=4)
        aks = sb("aks", [64, 2, 2, 64])
        Xp, Yp, Wp = part(4, P), part(4, P), part(4, P)
        Xs, Ys, Ws = sb("Xs", [64, 2, 64]), sb("Ys", [64, 2, 64]), sb("Ws", [64, 2, 64])
        tm = part(3, 5, P)
        p1 = sb("p1", [P, 2, P])
        u0 = sb("u0", [P, 2, P])
        bex, u0x, vx, gt = (scratch3[:, j * 1024:j * 1024 + 1024].rearrange("p (t c k) -> p t c k", t=2, c=4) for j in range(4))
        gt = gt.rearrange("p t c k -> p (t c) k")
        pus = sb("pus", [64, 2, P])
        rs = part(2, N)
        Sst = part(NCH + 1, P)
        s0raw = sb("s0raw", [64, NB, P])
        s0T = scratch2[:, 2048:2560].rearrange("p (b v) -> p b v", b=NB)
        ysm = sb("ysm", [P, 2, NB, TB])
        usb = sb("usb", [64, 2, HEAD])
        uex = scratch2[0:64, 0:1024].rearrange("p (h c) -> p h c", h=2)
        vex = scratch2[0:64, 1024:2048].rearrange("p (h c) -> p h c", h=2)
        s1T = scratch2[:, 2560:3072].rearrange("p (b v) -> p b v", b=NB)
        so_s = sb("so_s", [64, NB, P])
        so_p = sb("so_p", [P, HEAD])
        rowst = sb("rowst", [P, 12])

        xflat = xnT[:].rearrange("p k n -> p (k n)")
        mflat = merged[:].rearrange("p k n -> p (k n)")
        wo = [wall[:, j * D:j * D + D] for j in range(7)] + [xflat[:, D:2 * D]]
        x1 = wkv[:, 0:3 * D].rearrange("p (t d) -> p t d", t=3)
        xn2 = wkv[:, 3 * D:6 * D].rearrange("p (t d) -> p t d", t=3)
        norm2b = scratch2[:, 2 * D:3 * D]
        xn2T = xnT
        wgu = [w.rearrange("p (g k f) -> p g k f", g=2, k=KC) for w in
               (vecs[:, 0:4096], scratch[:, :], wall[:, 0:4096], scratch3[:, :])]
        wdn = [w.rearrange("p (j d) -> p j d", j=2) for w in
               (vecs[:, 4096:6144], scratch2[:, 0:2048], wall[:, 4096:6144], vecs[:, 6144:8192])]
        xg = [mflat[0:CAP, 0:D], mflat[0:CAP, D:2 * D], xflat[0:CAP, 0:D], xflat[0:CAP, D:2 * D]]
        xgT = scratch2[:, 2048:3072].rearrange("p (b k s) -> p b k s", b=2, k=KC)
        ye = vecs[:, 8192:9216].rearrange("p (b d) -> p b d", b=2)
        th, hh, hT = (vecs[:, 9216 + 128 * j:9344 + 128 * j] for j in range(3))
        ya = [wall[:, 0:3 * D].rearrange("p (t d) -> p t d", t=3), scratch[:, 0:3 * D].rearrange("p (t d) -> p t d", t=3)]
        fnb = vecs[:, 0:D]
        rw = sb("rw", [P, KC, NG + NE])
        rb = sb("rb", [NG + NE, 1])
        lgT = sb("lgT", [NG + NE, N])
        lg = sb("lg", [P, 3, NG + NE])
        r1 = sb("r1", [P, 3, 24])
        dg, cg, ohg = sb("dg", [P, 3, NG]), sb("cg", [P, 3, NG]), sb("ohg", [P, 3, NG])
        le, leg, cand = sb("le", [P, 3, NE_G, NG]), sb("leg", [P, 3, NE_G]), sb("cand", [P, 3, NE_G])
        oh = [sb("oh1", [P, 3, NE_G]), sb("oh2", [P, 3, NE_G])]
        OH = [sb("OH1", [P, 3, NG, NE_G]), sb("OH2", [P, 3, NG, NE_G])]
        Mk, slot = sb("Mk", [P, 3, NE]), sb("slot", [P, 3, NE])
        cnt, xe, incl, exb = (sb(n, [P, NE]) for n in ("cnt", "xe", "incl", "exb"))
        le9 = ams[0:1].rearrange("p a b -> p (a b)")[:, 0:NOV * NE].rearrange("p (j e) -> p j e", j=NOV)
        ovf = sb("ovf", [1, 16])
        ovi = sb("ovi", [1, 16], I32)
        slotu = sb("slotu", [P, 2, 3], U32)
        ids = sb("ids_sb", [P, 3])
        zu = sb("zu", [P, 32])
        tabr = ams[0:NE + NOV].rearrange("p a b -> p (a b)")[:, 448:448 + CAP]
        idx = sb("idx", [CAP, NE + NOV], U32)
        idxo = sb("idxo", [CAP, 1], U32)
        xn2d = nc.dram_tensor("xn2d", (N, D), F32, kind="Internal").ap()
        tab = nc.dram_tensor("tab", (ROWS, 1), F32, kind="Internal").ap()
        ybuf = nc.dram_tensor("ybuf", (ROWS, D), F32, kind="Internal").ap()
        zrow = Sst[0:64, 0:8, :].rearrange("p a b -> p (a b)")

        block = ctx.enter_context(nc.Block())

        def vcol(name, i, j=0):
            return vT[:, bass.ds(i + (VEC[name] + j), 1)]

        def tpbank(name):
            return bank[TPN[name] % 2][:, 0:N]

        def tp_ready(eng, i, name):
            eng.wait_ge(S("tp"), i * NTP + (TPN[name] + 1))

        def taken(eng, i, name):
            j = TPN[name]
            e = TP[j][1]
            n = sum(x == e for _, x in TP[:j + 1])
            eng.wait_ge(S("taken_" + e), i * (NTPA if e == "a" else NTPD) + n)

        def seq(ap, at, pad, a0, a1):
            return ap[:, at:at + NB * (pad + TB)].rearrange("p (b t) -> p b t", b=NB)[:, :, a0:a1]

        def s88(ap):
            return ap.rearrange("p (b t) -> p b t", b=NB)

        w_in = a["w_in"][0].rearrange("(k p) n -> p k n", p=P)

        @block.sync
        def _(sp):
            sp.dma_start(xt[:, 0:2, :], a["x_prompt"][0].rearrange("(t p) d -> p t d", p=P)).then_inc(S("x_in"), 16)
            sp.dma_start(xt[0:64, 2, :], a["x_sample"].rearrange("b t d -> (b t) d")).then_inc(S("x_in"), 16)
            sp.dma_start(consts[:], a["consts"]).then_inc(S("const_in"), 16)
            for name, key in (("conv_w", "conv_w"), ("conv_b", "conv_b"), ("lru_bx", "lru_bx"), ("lru_ba", "lru_ba"),
                              ("a_param", "lru_a_param"), ("w0", "rwkv_w0"), ("a0", "rwkv_a0"), ("k_k", "rwkv_k_k"),
                              ("k_a", "rwkv_k_a"), ("r_k", "rwkv_r_k"), ("ln_w", "rwkv_ln_w"), ("ln_b", "rwkv_ln_b"),
                              ("norm1", "norm1")):
                src, n = a[key], 8
                if key == "conv_w":
                    src, n = src.rearrange("o j (c p) -> (o j c) p", p=P), 32
                elif key == "rwkv_r_k":
                    src = src.rearrange("o (c h) k -> (o c) (h k)", h=2)
                else:
                    src = src.rearrange("o (c p) -> (o c) p", p=P)
                sp.dma_start(vrows[VEC[name]:VEC[name] + n, :], src).then_inc(S("vec_in"), 16)
            sp.dma_start(strows[0:24, :], a["state_conv"].rearrange("o b j d -> (o b j) d")).then_inc(S("vec_in"), 16)
            sp.dma_start(strows[24:32, :], a["state_lru"][0]).then_inc(S("vec_in"), 16)
            sp.dma_start(shrows, a["state_shift"][0]).then_inc(S("vec_in"), 16)
            sp.wait_ge(S("zeroed"), 1)
            sp.dma_start(murows[0:26, :], a["rwkv_mu"][0, 0:26 * P].rearrange("(c p) -> c p", p=P)).then_inc(S("vec_in"), 16)
            sp.dma_start(murows[26:27, 0:32], a["rwkv_mu"][:, 26 * P:RWKV]).then_inc(S("vec_in"), 16)
            sp.dma_start(ids[:], a["ids"]).then_inc(S("rt_in"), 16)
            sp.dma_start(rw[:, :, 0:NG], a["router_group"][0].rearrange("(k p) g -> p k g", p=P)).then_inc(S("rt_in"), 16)
            sp.dma_start(rw[:, :, NG:], a["router_expert"][0].rearrange("(k p) g -> p k g", p=P)).then_inc(S("rt_in"), 16)
            sp.dma_start(rb[0:NG, :], a["router_group_b"].rearrange("o g -> g o")).then_inc(S("rt_in"), 16)
            sp.dma_start(rb[NG:, :], a["router_expert_b"].rearrange("o g -> g o")).then_inc(S("rt_in"), 16)
            sp.wait_ge(S("zrow"), 1)
            sp.dma_start(tab[0:NE * CAP, :].rearrange("(p c) o -> p (c o)", p=P), zu[:, 0:NE * CAP // P]).then_inc(S("z_tab"), 16)
            sp.dma_start(tab[NE * CAP:ROWS, :].rearrange("(p c) o -> p (c o)", p=CAP), zu[0:CAP, 0:NOV]).then_inc(S("z_tab"), 16)
            for j in range(NOV):
                sp.dma_start(ybuf[(NE + j) * CAP:(NE + j + 1) * CAP, :], zrow).then_inc(S("z_out"), 16)
            sp.dma_start(wbuf["lx"][:], w_in[:, :, 5 * D:5 * D + 128]).then_inc(S("w_pre"), 16)
            sp.dma_start(wbuf["ly"][:], w_in[:, :, 5 * D + 128:5 * D + 256]).then_inc(S("w_pre"), 16)
            sp.dma_start(wbuf["gl"][:, :, 0:32], w_in[:, :, 5 * D + 256:5 * D + 288]).then_inc(S("w_pre"), 16)

            def pair_loads(i, first):
                at = i * P
                for n in ["r", "k", "v", "ly", "lx", "gl", "gr"]:
                    src = w_in[:, :, bass.ds(at + COL[n], P)]
                    if not first and n != "lx":
                        sp.wait_ge(S("tp"), i * NTP + (TPN[n] + 1 - NTP))
                    elif first and n == "ly":
                        sp.wait_ge(S("pre_mm"), 3)
                    sp.dma_start(wbuf[n][:], src).then_inc(S("w_" + n), 16)
                heads = a["state_wkv"][0].rearrange("b (q h) v k -> h v b q k", h=2)
                srcs = [heads[h, :, :, bass.ds(i, 1), :].rearrange("v b q k -> v b (q k)") for h in range(2)]
                if not first:
                    sp.wait_ge(S("s0t"), i)
                for h in range(2):
                    sp.dma_start(s0raw[:, :, HEAD * h:HEAD * h + HEAD], srcs[h]).then_inc(S("s0_in"), 16)
                if not first:
                    sp.wait_ge(S("tp"), i * NTP + (TPN["g"] + 1 - NTP))
                for dst, src in ((w2a2[0:64, :], a["rwkv_w2"][0, :, bass.ds(at, P)]),
                                 (w2a2[64:128, :], a["rwkv_a2"][0, :, bass.ds(at, P)]),
                                 (g2a[:], a["rwkv_g2"][0, 0:128, bass.ds(at, P)]),
                                 (g2b[:], a["rwkv_g2"][0, 128:160, bass.ds(at, P)]),
                                 (wxa[:, 0, :], a["lru_wx"][0].rearrange("n d e -> d n e")[:, bass.ds(i, 1), :].rearrange("d n e -> d (n e)")),
                                 (wxa[:, 1, :], a["lru_wa"][0].rearrange("n d e -> d n e")[:, bass.ds(i, 1), :].rearrange("d n e -> d (n e)"))):
                    sp.dma_start(dst, src).then_inc(S("small_in"), 16)

            pair_loads(0, True)
            with sp.Fori(1, PAIRS) as i:
                pair_loads(i, False)
            for j, n in enumerate(COL):
                sp.wait_ge(S("tp"), NTP * (PAIRS - 1) + TPN[n] + 1)
                sp.dma_start(wo[j], a["w_out"][0, j * P:j * P + P, :]).then_inc(S("w_" + n), 16)
            sp.dma_start(wo[7], a["w_out"][0, 7 * P:8 * P, :]).then_inc(S("wo_in"), 16)
            sp.wait_ge(S("merged"), PAIRS)
            sp.wait_ge(S("sout"), PAIRS)
            sp.dma_start(x1[:, 0:2, :], a["x_prompt"][0].rearrange("(t p) d -> p t d", p=P)).then_inc(S("x1_in"), 16)
            sp.dma_start(x1[0:64, 2, :], a["x_sample"].rearrange("b t d -> (b t) d")).then_inc(S("x1_in"), 16)
            sp.dma_start(norm2b, a["norm2"].broadcast_to([P, D])).then_inc(S("x1_in"), 16)

            def gu_src(name, e):
                return a[name][0].rearrange("e (p k) f -> p e (k f)", k=KC)[:, bass.ds(e, 1), :].rearrange("p e x -> p (e x)")

            def dn_src(e):
                return a["exp_down"][0].rearrange("e (j p) d -> p e j d", p=P)[:, bass.ds(e, 1)].rearrange("p e j d -> p (e j) d")

            def weights(j, e, sem):
                for g, name in enumerate(("exp_gate", "exp_up")):
                    sp.dma_start(wgu[j][:, g].rearrange("p k f -> p (k f)"), gu_src(name, e)).then_inc(S(sem), 16)
                sp.dma_start(wdn[j], dn_src(e)).then_inc(S(sem), 16)

            weights(0, 0, "ew0")
            weights(1, 1, "ew1")
            sp.wait_ge(S("wo_ps"), 1)
            weights(2, 2, "ew2")
            sp.wait_ge(S("rows_out"), 6 * 16)
            weights(3, 3, "ew3")
            with sp.Fori(1, NE // 4) as i:
                for j in range(4):
                    sp.wait_ge(S("dn"), i * 4 + (j - 3))
                    weights(j, i * 4 + j, f"ew{j}")
            sp.wait_ge(S("ov"), 1)
            n_ov = sp.value_load(ovi[0:1, NOV:NOV + 1], min_val=0, max_val=NOV)
            with sp.If(n_ov > 0):
                with sp.Fori(0, NOV) as j:
                    e = sp.value_load(ovi[0:1, bass.ds(j, 1)], min_val=0, max_val=NE - 1)
                    sp.wait_ge(S("dn"), j + NE)
                    if True:
                        weights(0, e, "ew0")
            sp.wait_ge(S("fin0"), 1)
            sp.dma_start(fnb, a["final_norm"].rearrange("(a d) -> a d", a=1).broadcast_to([P, D])).then_inc(S("fn_in"), 16)
            sp.wait_ge(S("y_fin"), 3)
            sp.dma_start(o["y_p"][0].rearrange("(t p) d -> p t d", p=P), x1[:, 0:2, :]).then_inc(S("stored"), 16)
            sp.dma_start(o["y_s"].rearrange("b t d -> (b t) d"), x1[0:64, 2, :]).then_inc(S("stored"), 16)
            sp.wait_ge(S("stored"), 32)

        @block.gpsimd
        def _(pool):
            def pair(i, first):
                pool.wait_ge(S("am"), i + 1)
                if not first:
                    pool.wait_ge(S("lvW"), i * 4)
                for k in range(4):
                    q = nc.gpsimd.tensor_tensor(ak[:, k], am[:, :, 0:128],
                                                lev[:, k + 1, None, :].broadcast_to([P, 4, P]), ALU.mult)
                    if k < 2:
                        q = nc.gpsimd.tensor_tensor(aks[:, k], ams[:, :, 0:64],
                                                    lev[0:64, k + 1, None, 0:64].broadcast_to([64, 2, 64]), ALU.mult)
                    q.then_inc(S("ak"), 1)
                pool.wait_ge(S("tm"), i * 3 + 3)
                if not first:
                    pool.wait_ge(S("su"), i)
                for h in range(2):
                    q = nc.gpsimd.tensor_tensor(
                        vex[:, h].rearrange("p (b v) -> p b v", b=NB),
                        tm[0:64, 2, 3, None, HEAD * h:HEAD * h + HEAD].broadcast_to([64, NB, HEAD]),
                        C("bm")[0:64, :, None].broadcast_to([64, NB, HEAD]), ALU.mult)
                q.then_inc(S("vex"), 1)
                if not first:
                    pool.wait_ge(S("y_ps"), i)
                for t in range(2):
                    nc.gpsimd.tensor_tensor(bex[:, t], tm[:, t, 1, None, :].broadcast_to([P, 4, P]),
                                            C("cm")[:, :, None].broadcast_to([P, 4, P]), ALU.mult).then_inc(S("bex"), 1)
                for t in range(2):
                    q = nc.gpsimd.tensor_tensor(vx[:, t], tm[:, t, 3, None, :].broadcast_to([P, 4, P]),
                                                C("cm")[:, :, None].broadcast_to([P, 4, P]), ALU.mult)
                q.then_inc(S("vx"), 1)
                for c in range(2):
                    pool.wait_ge(S("gtm"), i * 2 + (c + 1))
                    nc.gpsimd.tensor_tensor(gt[:, 4 * c:4 * c + 4], gt[:, 4 * c:4 * c + 4],
                                            ident[:, None, :].broadcast_to([P, 4, P]), ALU.add).then_inc(S("gt"), 1)

            pair(0, True)
            with pool.Fori(1, PAIRS) as i:
                pair(i, False)

            pool.wait_ge(S("slotu"), 1)
            pool.wait_ge(S("z_tab"), 32)
            pool.wait_ge(S("rt_in"), 16 * 5)
            for t, (_, n) in enumerate(TILES):
                for q in range(2):
                    pool.indirect_dma_start(tab, bass.IndirectOffsetOnAxis(ap=slotu[0:n, q, t:t + 1], axis=0),
                                            ids[0:n, t:t + 1], None).then_inc(S("tab"), 16)
            pool.wait_ge(S("tab"), 96)
            pool.dma_start(tabr, tab.rearrange("(e s) o -> e (s o)", s=CAP)).then_inc(S("tabr"), 16)
            pool.wait_ge(S("idx"), 1)
            pool.wait_ge(S("xn2d"), 48)

            def gather(j, e, sem):
                pool.indirect_dma_start(xg[j], None, xn2d, bass.IndirectOffsetOnAxis(ap=e, axis=0)).then_inc(S(sem), 16)

            for e in range(NE):
                if e == 2:
                    pool.wait_ge(S("lgT_ps"), 1)
                if e >= 4:
                    pool.wait_ge(S("gT_ps"), e - 3)
                gather(e % 4, idx[:, e:e + 1], f"xg{e % 4}")
            pool.wait_ge(S("ov"), 1)
            for j in range(2):
                pool.wait_ge(S(f"y_out{j}"), 16 * NE)

            def carry(cell):
                nc.gpsimd.tensor_tensor(ovf[0:1, cell:cell + 1], misc[0:1, 0:1], misc[0:1, 0:1], ALU.add).then_inc(S("o_idx"), 1)

            n_ov = pool.value_load(ovi[0:1, NOV:NOV + 1], min_val=0, max_val=NOV)
            with pool.If(n_ov > 0):
                with pool.Fori(0, NOV) as j:
                    pool.wait_ge(S("gT_ps"), j + NE)
                    carry(12)
                    nc.gpsimd.tensor_copy(idxo[:], idx[:, bass.ds(j + NE, 1)]).then_inc(S("o_idx"), 1)
                    pool.wait_ge(S("o_idx"), j * 3 + 2)
                    carry(13)
                    gather(0, idxo[:, 0:1], "xg0")
                pool.wait_ge(S("y_out0"), 16 * NE + 32 * NOV)
            pool.wait_ge(S("fin0"), 1)
            for t, (_, n) in enumerate(TILES):
                for q in range(2):
                    pool.indirect_dma_start(ya[q][0:n, t, :], None, ybuf,
                                            bass.IndirectOffsetOnAxis(ap=slotu[0:n, q, t:t + 1], axis=0))\
                        .then_inc(S(f"ya{t}"), 16)

        @block.tensor
        def _(pe):
            mm, tr = nc.tensor.matmul, nc.tensor.transpose
            pe.wait_ge(S("const_in"), 16)
            pe.wait_ge(S("vec_in"), 16 * 18)
            tr(bank[0][:, 0:128], vrows[:], ident)
            tr(bank[0][:, 128:128 + NMU], murows[:], ident[0:NMU, 0:NMU])
            for c in range(NMU):
                w = min(P, RWKV - c * P)
                tr(bank[1][0:w, 8 * c:8 * c + 8], shrows[:, c * P:c * P + w], ident[0:8, 0:8])
            for c in range(KC):
                q = tr(bank[2][:, 32 * c:32 * c + 32], strows[:, c * P:c * P + P], ident[0:32, 0:32])
            q.then_inc(S("vecT"), 1)
            for j in range(6):
                t, (_, n) = j // 2, TILES[j // 2]
                b = bank[3 + j % 2]
                pe.wait_ge(S("xn"), t + 1)
                if j >= 2:
                    pe.wait_ge(S("xnT"), j - 1)
                for c in range(4):
                    d = (4 * (j % 2) + c) * P
                    q = tr(b[:, c * P:c * P + n], xn[0:n, t, d:d + P], ident[0:n, 0:n])
                q.then_inc(S("xT_ps"), 1)
            pe.wait_ge(S("xnT"), 6)
            pe.wait_ge(S("w_pre"), 48)
            for j, (n, w) in enumerate((("lx", 128), ("ly", 128), ("gl", 32))):
                for k in range(KC):
                    q = mm(bank[5 + j][0:w, 0:N], wbuf[n][:, k, 0:w], xnT[:, k, :], start=(k == 0), stop=(k == KC - 1))
                q.then_inc(S("pre_mm"), 1)

            def pair(i, first):
                def room(name):
                    j = TPN[name] - 2
                    if j >= 0:
                        taken(pe, i, TP[j][0])
                    elif not first:
                        jj = j + NTP
                        e = TP[jj][1]
                        m = sum(x == e for _, x in TP[:jj + 1])
                        tot = NTPA if e == "a" else NTPD
                        pe.wait_ge(S("taken_" + e), i * tot + (m - tot))

                def proj(name):
                    room(name)
                    pe.wait_ge(S("w_" + name), i * 16 + 16)
                    for k in range(KC):
                        q = mm(tpbank(name), wbuf[name][:, k, :], xnT[:, k, :], start=(k == 0), stop=(k == KC - 1))
                    q.then_inc(S("tp"), 1)

                def single(name, lhsT, rhs):
                    room(name)
                    mm(tpbank(name), lhsT, rhs, start=True, stop=True).then_inc(S("tp"), 1)

                proj("r")
                proj("k")
                proj("v")
                pe.wait_ge(S("small_in"), i * 96 + 96)
                pe.wait_ge(S("lw"), 1)
                single("zw", w2a2[0:64, :], lw[0:64, 0, :])
                single("za", w2a2[64:128, :], lw[64:128, 0, :])
                proj("lx")
                pe.wait_ge(S("kk2"), i + 1)
                single("ss", blk, kk2[:])
                pe.wait_ge(S("rkk"), i + 1)
                single("bon", blk, rkk[:])
                proj("ly")
                pe.wait_ge(S("ops"), i + 1)
                pe.wait_ge(S("sout"), i)
                pe.wait_ge(S("merged"), i)
                for u in range(4):
                    t, h = u // 2, slice(64 * (u % 2), 64 * (u % 2) + 64)
                    cols = slice(128 * t, 128 * t + 128)
                    mm(bank[2 + u][:, 0:256], bt[h, cols], ar[h, :, cols], start=True, stop=True)
                    mm(bank[2 + u][:, 256:512], kt[h, cols], ar[h, :, cols], start=True, stop=True)\
                        .then_inc(S("big"), 1)
                for j in range(2):
                    h = slice(64 * j, 64 * j + 64)
                    mm(bank[6 + j][0:64, 0:128], bt[h, 256:N], ar[h, :, 256:N], start=True, stop=True)
                    q = mm(bank[6 + j][0:64, 128:256], kt[h, 256:N], ar[h, :, 256:N], start=True, stop=True)
                q.then_inc(S("big"), 1)
                for t, (t0, n) in enumerate(TILES):
                    if t == 0:
                        pe.wait_ge(S("am"), i + 1)
                    if t == 1:
                        pe.wait_ge(S("tm"), i * 3 + 1)
                    b = bank[2 if t == 1 else 7]
                    for j, src in enumerate((ar[:, 0, :], bt[:], kt[:], vm[:])):
                        q = tr(b[0:n, 128 * j:128 * j + 128], src[:, t0:t0 + n], ident)
                    q.then_inc(S("tm_ps"), 1)
                proj("gl")
                pe.wait_ge(S("y1"), i + 1)
                for u in range(4):
                    tr(bank[3][:, 128 * u:128 * u + 128], Yp[:, u, :], ident)
                for u in range(2):
                    q = tr(bank[4][0:64, 64 * u:64 * u + 64], Ys[:, u, :], ident[0:64, 0:64])
                q.then_inc(S("x1_ps"), 1)
                pe.wait_ge(S("tm"), i * 3 + 3)
                pe.wait_ge(S("s0_in"), i * 32 + 32)
                for u in range(4):
                    mm(bank[5][:, 128 * u:128 * u + 128], am[:, u, 256:384], tm[:, u // 2, 3, :], start=True, stop=True)
                for u in range(2):
                    q = mm(bank[6][0:64, 128 * u:128 * u + 128], ams[:, u, 128:192], tm[0:64, 2, 3, :], start=True, stop=True)
                q.then_inc(S("akv"), 1)
                for b in range(NB):
                    q = tr(bank[7][:, 64 * b:64 * b + 64], s0raw[:, b, :], ident[0:64, 0:64])
                q.then_inc(S("s0t"), 1)
                pe.wait_ge(S("xc"), i + 1)
                single("gx", wxa[:, 0, :], xc[:])
                single("ga", wxa[:, 1, :], xc[:])
                pe.wait_ge(S("x1"), i + 1)
                pe.wait_ge(S("akv_c"), i + 1)
                for k in range(4):
                    if k:
                        pe.wait_ge(S("lvl"), i * 4 + k)
                    pe.wait_ge(S("ak"), i * 4 + (k + 1))
                    small = k < 2
                    for u in range(4):
                        q = mm(bank[2][:, 128 * u:128 * u + 128], ak[:, k, u, :], Xp[:, u, :], start=True, stop=True)
                    for u in range(2 if small else 0):
                        q = mm(bank[6][0:64, 64 * u:64 * u + 64], aks[:, k, u, :], Xs[:, u, :], start=True, stop=True)
                    q.then_inc(S("lvW"), 1)
                    if k == 1:
                        proj("gr")
                    if k == 2:
                        room("g")
                        mm(tpbank("g"), g2a[:], lw[:, 1, :], start=True, stop=False)
                        mm(tpbank("g"), g2b[:], lw[0:32, 2, :], start=False, stop=True).then_inc(S("tp"), 1)
                    pe.wait_ge(S("lvWc"), i * 4 + (k + 1))
                    for u in range(4 if k < 3 else 0):
                        mm(bank[3][:, 128 * u:128 * u + 128], Yp[:, u, :], Wp[:, u, :], start=True, stop=True)
                    for u in range(4):
                        q = mm(bank[4][:, 128 * u:128 * u + 128], Wp[:, u, :], Yp[:, u, :], start=True, stop=True)
                    for u in range(2 if small else 0):
                        mm(bank[6][0:64, 128 + 64 * u:192 + 64 * u], Ys[:, u, :], Ws[:, u, :], start=True, stop=True)
                        q = mm(bank[6][0:64, 256 + 64 * u:320 + 64 * u], Ws[:, u, :], Ys[:, u, :], start=True, stop=True)
                    q.then_inc(S("lvM"), 1)
                pe.wait_ge(S("lvl"), i * 4 + 4)
                pe.wait_ge(S("s0c"), i + 1)
                for u in range(4):
                    c = 64 * (u % 2)
                    mm(bank[2][:, 128 * u:128 * u + 128], Yp[:, u, :], tm[:, u // 2, 0:5:4, c:c + 64], start=True, stop=True)
                for u in range(2):
                    c = 64 * u
                    mm(bank[6][0:64, 256 + 128 * u:384 + 128 * u], Ys[:, u, :], tm[0:64, 2, 0:5:4, c:c + 64], start=True, stop=True)
                    q = mm(bank[7][c:c + 64, 0:64], tm[0:64, 2, 0, c:c + 64], Ys[:, u, :], start=True, stop=True)
                q.then_inc(S("pu_ps"), 1)
                pe.wait_ge(S("pu"), i + 1)
                pe.wait_ge(S("bex"), i * 2 + 1)
                mm(bank[5][:], p1[:, 0, :], bex[:, 0].rearrange("p c k -> p (c k)"), start=True, stop=True).then_inc(S("gt_ps"), 1)
                pe.wait_ge(S("u0x"), i * 2 + 2)
                pe.wait_ge(S("bex"), i * 2 + 2)
                mm(bank[2][:], p1[:, 1, :], bex[:, 1].rearrange("p c k -> p (c k)"), start=True, stop=True).then_inc(S("gt_ps"), 1)
                for h in range(2):
                    c = slice(64 * h, 64 * h + 64)
                    for t in range(2):
                        mm(bank[3][c, 128 * t:128 * t + 128], p1[:, t, c], am[:, 2 * t + h, 128:256], start=True, stop=True)
                    q = mm(bank[3][c, 256:N], pus[:, h, 0:64], ams[:, h, 64:128], start=True, stop=True)
                q.then_inc(S("rh_ps"), 1)
                for h in range(2):
                    c = slice(64 * h, 64 * h + 64)
                    for t in range(2):
                        u = 2 * t + h
                        mm(bank[4][c, 128 * t:128 * t + 128], u0[:, t, c], am[:, u, 128:256], start=(t == 0), stop=False,
                           skip_group_check=True)
                        mm(bank[4][c, 128 * t:128 * t + 128], tm[:, t, 3, c], am[:, u, 384:512], start=False, stop=True,
                           skip_group_check=True)
                    mm(bank[4][c, 256:N], pus[:, h, 64:128], ams[:, h, 64:128], start=False, stop=False, skip_group_check=True)
                    mm(bank[4][c, 256:N], tm[0:64, 2, 3, c], ams[:, h, 192:256], start=False, stop=True, skip_group_check=True)
                for t, b in ((0, bank[7]), (1, bank[3])):
                    if t == 0:
                        pe.wait_ge(S("vx"), i + 1)
                    else:
                        pe.wait_ge(S("rhat"), i + 1)
                    mm(b[:], tm[:, t, 1, :], u0x[:, t].rearrange("p c k -> p (c k)"), start=True, stop=False,
                       skip_group_check=True)
                    q = mm(b[:], tm[:, t, 2, :], vx[:, t].rearrange("p c k -> p (c k)"), start=False, stop=True,
                           skip_group_check=True)
                    if t == 0:
                        q.then_inc(S("st_ps"), 1)
                for c in range(1, NCH):
                    t = c // 4
                    if c % 4 == 0 or c == 1:
                        pe.wait_ge(S("gt"), i * 2 + (1 + c // 4))
                    pe.wait_ge(S("state"), i * NCH + c)
                    mm(bank[7 if t == 0 else 3][:, 128 * (c % 4):128 * (c % 4) + 128], gt[:, c, :], Sst[:, c, :], start=False,
                       stop=True, skip_group_check=True).then_inc(S("st_ps"), 1)
                    q = mm(bank[4][:, CH * c:CH * c + CH], Sst[:, c, :], rs[:, 1, CH * c:CH * c + CH], start=False,
                           stop=True, skip_group_check=True)
                q.then_inc(S("y_ps"), 1)
                for b in range(NB):
                    for h in range(2):
                        c = slice(64 * h, 64 * h + 64)
                        q = mm(bank[6][c, 16 * b:16 * b + 16], s0T[c, b, :], rs[c, :, 256 + TB * b:256 + TB * b + TB],
                               start=True, stop=True)
                q.then_inc(S("sm_ps"), 1)
                pe.wait_ge(S("ysm"), i + 1)
                pe.wait_ge(S("yT"), i + 1)
                single("mean", C("blkmean"), yT[:])
                tr(bank[6][0:64, 128:256], ysm[:, 0].rearrange("p b t -> p (b t)"), ident).then_inc(S("u_ps"), 1)
                pe.wait_ge(S("state"), i * NCH + NCH)
                pe.wait_ge(S("uex"), i + 1)
                pe.wait_ge(S("vex"), i + 1)
                tr(bank[5][:, 0:128], Sst[:, NCH, :], ident)
                for h in range(2):
                    c = slice(64 * h, 64 * h + 64)
                    mm(bank[6][c, :], tm[0:64, 2, 1, c], uex[:, h, :], start=True, stop=False)
                    q = mm(bank[6][c, :], tm[0:64, 2, 2, c], vex[:, h, :], start=False, stop=True)
                q.then_inc(S("su"), 1)
                pe.wait_ge(S("supd"), i + 1)
                pe.wait_ge(S("yc2"), i + 1)
                single("var", C("blkmean"), yc2[:])
                for b in range(NB):
                    q = tr(bank[2 + 5 * (b // 4)][0:64, 128 * (b % 4):128 * (b % 4) + 128], s1T[:, b, :], ident)
                q.then_inc(S("so_ps"), 1)

            pair(0, True)
            with pe.Fori(1, PAIRS) as i:
                pair(i, False)
            ob = [bank[j] for j in (0, 3, 4, 6, 2, 7)]
            pe.wait_ge(S("sout"), PAIRS)
            for k in range(KC):
                if k < 7:
                    pe.wait_ge(S("w_" + list(COL)[k]), 16 * PAIRS + 16)
                else:
                    pe.wait_ge(S("wo_in"), 16)
                if k == KC - 1:
                    pe.wait_ge(S("merged"), PAIRS)
                for t, (t0, n) in enumerate(TILES):
                    for h in range(2):
                        q = mm(ob[2 * t + h][0:n, :], merged[:, k, t0:t0 + n], wo[k][:, 512 * h:512 * h + 512],
                               start=(k == 0), stop=(k == KC - 1))
                        if k == KC - 1 and t < 2 and h == 1:
                            q.then_inc(S("o_ps"), 1)
            q.then_inc(S("wo_ps"), 1)
            for c in range(KC):
                q = tr(bank[1 if c < 4 else 5][0:36, 128 * (c % 4):128 * (c % 4) + 128], lastL[:, c, :], ident)
            q.then_inc(S("rowL_ps"), 1)
            for c in range(NMU):
                w = min(P, RWKV - c * P)
                g = c // 4
                if c % 4 == 0:
                    pe.wait_ge(S("rowP_c"), max(g, 1))
                q = tr(bank[5 if g % 2 else 1][0:9, 128 * (c % 4):128 * (c % 4) + w], lastP[0:w, c, :], ident[0:w, 0:w])
                if c % 4 == 3 or c == NMU - 1:
                    q.then_inc(S("rowP_ps"), 1)
            for j in range(6):
                t, (_, n) = j // 2, TILES[j // 2]
                pe.wait_ge(S("xn2"), t + 1)
                if j >= 2:
                    pe.wait_ge(S("xn2T"), j - 1)
                for c in range(4):
                    d = (4 * (j % 2) + c) * P
                    q = tr(bank[2 + j % 2][:, c * P:c * P + n], xn2[0:n, t, d:d + P], ident[0:n, 0:n])
                q.then_inc(S("x2T_ps"), 1)
            pe.wait_ge(S("rt_in"), 16 * 5)
            pe.wait_ge(S("xn2T"), 6)
            for k in range(KC):
                q = mm(bank[4][0:NG + NE, 0:N], rw[:, k, :], xn2T[:, k, :], start=(k == 0), stop=(k == KC - 1))
            q.then_inc(S("lgT_ps"), 1)
            pe.wait_ge(S("lgT"), 1)
            for t, (t0, n) in enumerate(TILES):
                q = tr(bank[5][0:n, 64 * t:64 * t + NG + NE], lgT[:, t0:t0 + n], ident[0:NG + NE, 0:NG + NE])
            q.then_inc(S("lg_ps"), 1)
            pe.wait_ge(S("Mk"), 1)
            ones, tri = C("ones"), C("tri")
            for t, (_, n) in enumerate(TILES):
                for u in range(t):
                    mm(bank[6][0:n, 32 * t:32 * t + 32], ones[:, 0:n], Mk[:, u, :], start=(u == 0), stop=False)
                mm(bank[6][0:n, 32 * t:32 * t + 32], tri[0:n, 0:n], Mk[0:n, t, :], start=(t == 0), stop=True)
            for u, (_, n) in enumerate(TILES):
                q = mm(bank[7][:, 0:32], ones[0:n, :], Mk[0:n, u, :], start=(u == 0), stop=(u == 2))
            q.then_inc(S("cnt_ps"), 1)

            pe.wait_ge(S("tabr"), 16)
            tr(bank[1][0:CAP, 0:NE + NOV], tabr, ident[0:NE + NOV, 0:NE + NOV]).then_inc(S("idx_ps"), 1)

            def T(b, src):
                for k in range(KC):
                    q = tr(b[:, CAP * k:CAP * k + CAP], src[:, k:D:KC], ident[0:CAP, 0:CAP])
                return q

            def GU(b, xT, w):
                for k in range(KC):
                    for f in range(2):
                        q = mm(b[64 * f:64 * f + 64, 0:256], xT[:, k, :], w[:, :, k, 128 * f:128 * f + 128],
                               start=(k == 0), stop=(k == KC - 1))
                return q

            def DN(b, w):
                for j in range(2):
                    for d in range(2):
                        q = mm(b[64 * d:64 * d + 64, :], hT[:, 64 * j:64 * j + 64], w[:, j, 512 * d:512 * d + 512],
                               start=(j == 0), stop=(j == 1))
                return q

            def experts(i, first, last):
                for j in range(4):
                    nxt, b = (j + 1) % 4, (j + 1) % 2
                    if not (last and j == 3):
                        pe.wait_ge(S(f"xg{nxt}"), i * 16 + 16 * (1 + (j + 1) // 4))
                    pe.wait_ge(S(f"ew{j}"), i * 48 + 48)
                    pe.wait_ge(S("gT"), i * 4 + (j + 1))
                    if not (first and j < 2):
                        pe.wait_ge(S("h"), i * 4 + (j - 1))
                    GU(bank[2 + j % 2], xgT[:, j % 2], wgu[j]).then_inc(S("gu"), 1)
                    if not (last and j == 3):
                        pe.wait_ge(S("idx"), 1)
                        T(bank[b], xg[nxt]).then_inc(S("gT_ps"), 1)
                    if not (first and j == 0):
                        pe.wait_ge(S("hT"), i * 4 + j)
                        if not (first and j < 3):
                            pe.wait_ge(S("ye"), i * 4 + (j - 2))
                        DN(bank[6 + b], wdn[(j - 1) % 4]).then_inc(S("dn"), 1)
                    pe.wait_ge(S("h"), i * 4 + (j + 1))
                    tr(bank[4][:, 0:128], hh, ident).then_inc(S("hT_ps"), 1)

            pe.wait_ge(S("slotu"), 1)
            pe.wait_ge(S("xg0"), 16)
            T(bank[0], xg[0]).then_inc(S("gT_ps"), 1)
            experts(0, True, False)
            with pe.Fori(1, NE // 4 - 1) as i:
                experts(i, False, False)
            experts(NE // 4 - 1, False, True)
            pe.wait_ge(S("hT"), NE)
            pe.wait_ge(S("ye"), NE - 2)
            DN(bank[7], wdn[3]).then_inc(S("dn"), 1)
            pe.wait_ge(S("ov"), 1)
            n_ov = pe.value_load(ovi[0:1, NOV:NOV + 1], min_val=0, max_val=NOV)
            with pe.If(n_ov > 0):
                with pe.Fori(0, NOV) as j:
                    pe.wait_ge(S("xg0"), j * 16 + 16 * (NE // 4 + 1))
                    pe.wait_ge(S("ye"), j + NE)
                    mm(bank[5][:, 0:128], ident, ident, start=True, stop=True)
                    T(bank[0], xg[0]).then_inc(S("gT_ps"), 1)
                    pe.wait_ge(S("ew0"), j * 48 + 48 * (NE // 4 + 1))
                    pe.wait_ge(S("gT"), j + (NE + 1))
                    mm(bank[5][:, 0:128], ident, ident, start=True, stop=True)
                    GU(bank[2], xgT[:, 0], wgu[0]).then_inc(S("gu"), 1)
                    pe.wait_ge(S("h"), j + (NE + 1))
                    tr(bank[4][:, 0:128], hh, ident).then_inc(S("hT_ps"), 1)
                    pe.wait_ge(S("hT"), j + (NE + 1))
                    mm(bank[5][:, 0:128], ident, ident, start=True, stop=True)
                    DN(bank[6], wdn[0]).then_inc(S("dn"), 1)

        @block.scalar
        def _(act):
            A = nc.scalar.activation
            for t, (_, n) in enumerate(TILES):
                act.wait_ge(S("x_in"), 32)
                if t == 0:
                    act.wait_ge(S("const_in"), 16)
                A(xn[0:n, t, :], xt[0:n, t, :], ACT.Square, accum_out=rowst[0:n, t:t + 1]).then_inc(S("sumsq"), 1)
            act.wait_ge(S("sumsq"), 3)
            for t, (_, n) in enumerate(TILES):
                A(rowst[0:n, 3 + t:4 + t], rowst[0:n, t:t + 1], ACT.Sqrt, bias=misc[0:n, 2:3], scale=1.0 / D).then_inc(S("rms"), 1)
            act.wait_ge(S("vecc"), 1)
            A(lst[:, 0, :], vT[:, VEC["a_param"]:VEC["a_param"] + 8], ACT.Abs).then_inc(S("lsa"), 1)
            act.wait_ge(S("lsa"), 1)
            A(lst[:, 1, :], lst[:, 0, :], ACT.Exp, scale=-1.0).then_inc(S("lsa"), 1)
            act.wait_ge(S("lsa"), 2)
            A(lst[:, 2, :], lst[:, 1, :], ACT.Ln, bias=misc[:, 3:4]).then_inc(S("lsa"), 1)
            for j, (n, w) in enumerate((("r", 128), ("k", 128), ("v", 32))):
                act.wait_ge(S("pre_mm"), j + 1)
                act.wait_ge(S("padz"), 1)
                A(pad1[n][0:w, 1:257], bank[5 + j][0:w, 0:256], ACT.Copy)
                A(seq(pad1[n], 257, 1, 1, 9)[0:w], s88(bank[5 + j][0:w, 256:N]), ACT.Copy).then_inc(S("pre_c"), 1)
            act.wait_ge(S("pre_mix"), 1)
            A(lw[0:64, 0, :], lw[0:64, 0, :], ACT.Tanh)
            A(lw[:, 1, :], lw[:, 1, :], ACT.Tanh, scale=0.5)
            A(lw[0:32, 2, :], lw[0:32, 2, :], ACT.Tanh, scale=0.5).then_inc(S("lwt"), 1)

            def pair(i, first):
                def evac_pad(name, buf, pad):
                    tp_ready(act, i, name)
                    A(buf[:, pad:pad + 256], tpbank(name)[:, 0:256], ACT.Copy)
                    A(seq(buf, pad + 256, pad, pad, pad + TB), s88(tpbank(name)[:, 256:N]), ACT.Copy).then_inc(S("taken_a"), 1)

                for n in "rkv":
                    act.wait_ge(S("mixed"), i * 3 + (1 + "rkv".index(n)))
                    evac_pad(n, pad1[n], 1)
                if not first:
                    act.wait_ge(S("merged"), i)
                tp_ready(act, i, "zw")
                A(tw[:], tpbank("zw"), ACT.Tanh, bias=half[:, bass.ds(i, 1)], scale=0.5).then_inc(S("taken_a"), 1)
                taken(act, i, "zw")
                A(dec[:], tw[:], ACT.Exp, bias=misc[:, 0:1], scale=-0.5 * E_M05).then_inc(S("dec"), 1)
                tp_ready(act, i, "za")
                A(ta[:], tpbank("za"), ACT.Tanh, bias=half[:, bass.ds(i + 8, 1)], scale=0.5).then_inc(S("taken_a"), 1)
                evac_pad("lx", pad3, 3)
                taken(act, i, "ss")
                A(nrm[:], nrm[:], ACT.Sqrt).then_inc(S("nrm"), 1)
                tp_ready(act, i, "ly")
                A(ysq[:], tpbank("ly"), ACT.Square)
                A(ysb[:], tpbank("ly"), ACT.Copy).then_inc(S("taken_a"), 1)
                for t in range(3):
                    n = TILES[t][1]
                    act.wait_ge(S("tm_ps"), i * 3 + (t + 1))
                    A(tm[0:n, t, 0:4, :], bank[2 if t == 1 else 7][0:n, :].rearrange("p (j c) -> p j c", j=4), ACT.Copy)\
                        .then_inc(S("tm"), 1)
                tp_ready(act, i, "gl")
                A(tgl[:], tpbank("gl"), ACT.Tanh, scale=0.5).then_inc(S("taken_a"), 1)
                act.wait_ge(S("x1_ps"), i + 1)
                A(Xp[:], bank[3][:].rearrange("p (u t) -> p u t", u=4), ACT.Copy)
                A(Xs[:], bank[4][0:64, 0:128].rearrange("p (u t) -> p u t", u=2), ACT.Copy).then_inc(S("x1"), 1)
                act.wait_ge(S("s0t"), i + 1)
                A(s0T[:], bank[7][:].rearrange("p (b v) -> p b v", b=NB), ACT.Copy).then_inc(S("s0c"), 1)
                tp_ready(act, i, "gx")
                A(tgx[:], tpbank("gx"), ACT.Tanh, bias=half[:, bass.ds(i + 16, 1)], scale=0.5).then_inc(S("taken_a"), 1)
                tp_ready(act, i, "ga")
                A(tga[:], tpbank("ga"), ACT.Tanh, bias=half[:, bass.ds(i + 24, 1)], scale=0.5).then_inc(S("taken_a"), 1)

                def level(k):
                    act.wait_ge(S("lvW"), i * 4 + (k + 1))
                    q = A(Wp[:], bank[2][:].rearrange("p (u t) -> p u t", u=4), ACT.Copy)
                    if k < 2:
                        q = A(Ws[:], bank[6][0:64, 0:128].rearrange("p (u t) -> p u t", u=2), ACT.Copy)
                    q.then_inc(S("lvWc"), 1)

                level(0)
                taken(act, i, "ga")
                A(la[:], tga[:], ACT.Exp, bias=ls4[:, bass.ds(i, 1)], scale=ls4[:, bass.ds(i, 1)])
                A(lth[:], tga[:], ACT.Tanh, bias=ls4[:, bass.ds(i, 1)], scale=ls4[:, bass.ds(i, 1)]).then_inc(S("la"), 1)
                level(1)
                act.wait_ge(S("u_gelu"), i + 1)
                A(tu[:], tu[:], ACT.Tanh, scale=0.7978845608028654).then_inc(S("tu"), 1)
                tp_ready(act, i, "gr")
                A(tgr[:], tpbank("gr"), ACT.Tanh, scale=0.5).then_inc(S("taken_a"), 1)
                level(2)
                act.wait_ge(S("m2"), i + 1)
                A(lm[:], lm[:], ACT.Sqrt).then_inc(S("lm"), 1)
                level(3)
                act.wait_ge(S("pu_ps"), i + 1)
                ps = bank[2][:].rearrange("p (t h x c) -> p t h x c", t=2, h=2, x=2)
                for t in range(2):
                    A(p1[:, t].rearrange("p (h c) -> p h c", h=2), ps[:, t, :, 0, :], ACT.Copy)
                    A(u0[:, t].rearrange("p (h c) -> p h c", h=2), ps[:, t, :, 1, :], ACT.Copy)
                A(pus[:], bank[6][0:64, 256:512].rearrange("p (u t) -> p u t", u=2), ACT.Copy)
                A(rs[:, 0, 256:N], bank[7][:, 0:64], ACT.Copy).then_inc(S("pu"), 1)
                act.wait_ge(S("sm_ps"), i + 1)
                A(ysm[:].rearrange("p x b t -> p b x t"), bank[6][:, 0:128].rearrange("p (b x t) -> p b x t", b=NB, x=2),
                  ACT.Copy).then_inc(S("ysm"), 1)
                taken(act, i, "mean")
                A(yc2[:], yc[:], ACT.Square).then_inc(S("yc2"), 1)
                act.wait_ge(S("so_ps"), i + 1)
                if not first:
                    act.wait_ge(S("wkv_out"), i * 48)
                A(so_p[0:64, :], bank[5][0:64, 0:64], ACT.Copy)
                A(so_p[64:128, :], bank[5][64:128, 64:128], ACT.Copy)
                for j in range(2):
                    q = A(so_s[:, 4 * j:4 * j + 4, :], bank[2 + 5 * j][0:64, :].rearrange("p (b c) -> p b c", b=4), ACT.Copy)
                q.then_inc(S("sout"), 1)
                act.wait_ge(S("sout"), i + 1)
                act.dma_start(o["wkv_p"][0, 0].rearrange("(q h) v k -> q (h v) k", h=2)[bass.ds(i, 1)]
                              .rearrange("q p k -> (q p) k"), so_p[:]).then_inc(S("wkv_out"), 16)
                for h in range(2):
                    act.dma_start(o["wkv_s"][0].rearrange("b (q h) v k -> h v b q k", h=2)[h, :, :, bass.ds(i, 1), :]
                                  .rearrange("v b q k -> v b (q k)"), so_s[:, :, 64 * h:64 * h + 64]).then_inc(S("wkv_out"), 16)
                tp_ready(act, i, "var")
                A(gns[:], tpbank("var"), ACT.Sqrt, bias=misc[:, 1:2]).then_inc(S("taken_a"), 1)

            pair(0, True)
            with act.Fori(1, PAIRS) as i:
                pair(i, False)
            act.wait_ge(S("rowL_ps"), 1)
            A(rowL[:, 0:512], bank[1][0:36, :], ACT.Copy)
            A(rowL[:, 512:1024], bank[5][0:36, :], ACT.Copy).then_inc(S("rowP_c"), 1)
            act.wait_ge(S("rowP_c"), 1)
            for dst, src in ((o["conv_p"][0, 0], rowL[0:3, :]), (o["conv_s"][0].rearrange("b j d -> (b j) d"), rowL[3:27, :]),
                             (o["lru_p"][0], rowL[27:28, :]), (o["lru_s"][0], rowL[28:36, :])):
                act.dma_start(dst, src).then_inc(S("rows_out"), 16)
            for g in range(7):
                w = min(512, RWKV - 512 * g)
                act.wait_ge(S("rowP_ps"), g + 1)
                A(rowP[:, 512 * g:512 * g + w], bank[5 if g % 2 else 1][0:9, 0:w], ACT.Copy).then_inc(S("rowP_c"), 1)
            act.wait_ge(S("rowP_c"), 8)
            for dst, src in ((o["shift_p"][0], rowP[0:1, 0:RWKV]), (o["shift_s"][0], rowP[1:9, 0:RWKV])):
                act.dma_start(dst, src).then_inc(S("rows_out"), 16)
            for t, (_, n) in enumerate(TILES):
                act.wait_ge(S("x1r"), t + 1)
                A(xn2[0:n, t, :], x1[0:n, t, :], ACT.Square, accum_out=rowst[0:n, t:t + 1]).then_inc(S("sumsq"), 1)
            act.wait_ge(S("sumsq"), 6)
            for t, (_, n) in enumerate(TILES):
                A(rowst[0:n, 3 + t:4 + t], rowst[0:n, t:t + 1], ACT.Sqrt, bias=misc[0:n, 2:3], scale=1.0 / D).then_inc(S("rms"), 1)
            for t, (t0, n) in enumerate(TILES):
                act.wait_ge(S("xn2"), t + 1)
                act.dma_start(xn2d[t0:t0 + n, :], xn2[0:n, t, :]).then_inc(S("xn2d"), 16)
            act.wait_ge(S("rows_out"), 96)
            for j in range(6):
                t, (t0, n) = j // 2, TILES[j // 2]
                act.wait_ge(S("x2T_ps"), j + 1)
                A(xn2T[:, 4 * (j % 2):4 * (j % 2) + 4, t0:t0 + n],
                  bank[2 + j % 2][:].rearrange("p (c t) -> p c t", c=4)[:, :, 0:n], ACT.Copy).then_inc(S("xn2T"), 1)
            act.wait_ge(S("lgT_ps"), 1)
            A(lgT[:], bank[4][0:NG + NE, 0:N], ACT.Identity, bias=rb[:, 0:1]).then_inc(S("lgT"), 1)
            act.wait_ge(S("dexp"), 1)
            A(dg[:], dg[:], ACT.Exp).then_inc(S("gexp"), 1)
            act.wait_ge(S("dexp"), 2)
            A(r1[:, :, 7:8], r1[:, :, 6:7], ACT.Exp).then_inc(S("gexp"), 1)

            yrows = ybuf.rearrange("(e s) d -> s e d", s=CAP)

            def yout(e, b):
                for d in range(2):
                    act.dma_start(yrows[:, bass.ds(e, 1), 512 * d:512 * d + 512].rearrange("s e d -> s (e d)"),
                                  ye[64 * d:64 * d + 64, b, :]).then_inc(S(f"y_out{b}"), 16)

            def xcols(b):
                A(xgT[:, b], bank[b][:].rearrange("p (k s) -> p k s", k=KC), ACT.Copy).then_inc(S("gT"), 1)

            def experts(i, first, last):
                for j in range(4):
                    act.wait_ge(S("gu"), i * 4 + (j + 1))
                    if not (first and j == 0):
                        act.wait_ge(S("h"), i * 4 + j)
                    A(th, bank[2 + j % 2][:, 0:128], ACT.Tanh, scale=0.5).then_inc(S("th"), 1)
                    if not (last and j == 3):
                        act.wait_ge(S("gT_ps"), i * 4 + (j + 2))
                        xcols((j + 1) % 2)
                    if not (first and j == 0):
                        act.wait_ge(S("ye"), i * 4 + j)
                        yout(i * 4 + (j - 1), (j - 1) % 2)
                        act.wait_ge(S("dn"), i * 4 + j)
                    act.wait_ge(S("hT_ps"), i * 4 + (j + 1))
                    A(hT, bank[4][:, 0:128], ACT.Copy).then_inc(S("hT"), 1)

            act.wait_ge(S("gT_ps"), 1)
            xcols(0)
            experts(0, True, False)
            with act.Fori(1, NE // 4 - 1) as i:
                experts(i, False, False)
            experts(NE // 4 - 1, False, True)
            act.wait_ge(S("ye"), NE)
            yout(NE - 1, 1)
            act.wait_ge(S("ov"), 1)
            act.wait_ge(S("y_out0"), 16 * NE)
            n_ov = act.value_load(ovi[0:1, NOV:NOV + 1], min_val=0, max_val=NOV)
            with act.If(n_ov > 0):
                with act.Fori(0, NOV) as j:
                    act.wait_ge(S("gT_ps"), j + (NE + 1))
                    A(xgT[:, 0], bank[0][:].rearrange("p (k s) -> p k s", k=KC), ACT.Copy).then_inc(S("gT"), 1)
                    act.wait_ge(S("gu"), j + (NE + 1))
                    A(th, bank[2][:, 0:128], ACT.Tanh, scale=0.5).then_inc(S("th"), 1)
                    act.wait_ge(S("hT_ps"), j + (NE + 1))
                    A(hT, bank[4][:, 0:128], ACT.Copy).then_inc(S("hT"), 1)
                    act.wait_ge(S("ye"), j + (NE + 1))
                    yout(j + NE, 0)
                act.wait_ge(S("y_out0"), 16 * NE + 32 * NOV)
            for t, (_, n) in enumerate(TILES):
                act.wait_ge(S("x2r"), t + 1)
                A(xn2[0:n, t, :], x1[0:n, t, :], ACT.Square, accum_out=rowst[0:n, t:t + 1]).then_inc(S("sumsq"), 1)
            act.wait_ge(S("sumsq"), 9)
            for t, (_, n) in enumerate(TILES):
                A(rowst[0:n, 3 + t:4 + t], rowst[0:n, t:t + 1], ACT.Sqrt, bias=misc[0:n, 2:3], scale=1.0 / D).then_inc(S("rms"), 1)
            act.wait_ge(S("wkv_out"), 48 * PAIRS)

        @block.vector
        def _(dve):
            TT, TS, STT, CP = nc.vector.tensor_tensor, nc.vector.tensor_scalar, nc.vector.scalar_tensor_tensor, nc.vector.tensor_copy
            MS = nc.vector.memset
            MUL, ADD, SUB, MAX, MIN = ALU.mult, ALU.add, ALU.subtract, ALU.max, ALU.min
            MS(murows[:], 0.0).then_inc(S("zeroed"), 1)
            for n in "rkv":
                MS(pad1[n][:, 0:1], 0.0)
            MS(wsh[:, 0:1], 0.0)
            MS(zu[:], 0.0)
            MS(zrow, 0.0).then_inc(S("zrow"), 1)
            MS(pad3[:, 0:3], 0.0).then_inc(S("padz"), 1)
            ch = Chain(dve, S("dve_pre"))
            for t, (_, n) in enumerate(TILES):
                dve.wait_ge(S("rms"), 3)
                ch.step(nc.vector.reciprocal(rowst[0:n, 6 + t:7 + t], rowst[0:n, 3 + t:4 + t]))
                TS(xn[0:n, t, :], xt[0:n, t, :], rowst[0:n, 6 + t:7 + t], None, MUL).then_inc(S("xn"), 1)
            dve.wait_ge(S("vecT"), 1)
            ch.go(CP(vT[:], bank[0][:, 0:128]))
            ch.go(CP(muT[:], bank[0][:, 128:128 + NMU]))
            ch.go(CP(shT[:, 0:26, :], bank[1][:, 0:208].rearrange("p (c b) -> p c b", b=8)))
            ch.go(CP(shT[0:32, 26, :], bank[1][0:32, 208:216]))
            CP(cvT[:], bank[2][:, 0:256].rearrange("p (c b) -> p c b", b=32)).then_inc(S("vecc"), 1)
            dve.wait_ge(S("vecc"), 1)
            for j, n in enumerate(("w0", "a0", "lru_bx", "lru_ba")):
                ch.go(TS(half[:, 8 * j:8 * j + 8], vT[:, VEC[n]:VEC[n] + 8], 0.5, None, MUL))
            for j in range(6):
                t, (t0, n) = j // 2, TILES[j // 2]
                dve.wait_ge(S("xT_ps"), j + 1)
                for c in range(4):
                    k = 4 * (j % 2) + c
                    q = TS(xnT[:, k, t0:t0 + n], bank[3 + j % 2][:, c * P:c * P + n], vT[:, VEC["norm1"] + k:VEC["norm1"] + k + 1],
                           None, MUL)
                q.then_inc(S("xnT"), 1)
            dve.wait_ge(S("lsa"), 3)
            ch.step(STT(lst[:, 0, :], vT[:, VEC["a_param"]:VEC["a_param"] + 8], 0.0, lst[:, 2, :], MIN, SUB))
            ch.go(TS(ls4[:], lst[:, 0, :], 4.0, None, MUL))

            def mix(ch, buf, w, chunk, out, fin=None):
                cc = chunk if not isinstance(chunk, int) else chunk
                ch.go(CP(seq(buf, 257, 1, 0, 1)[0:w].rearrange("p b t -> p t b"), shT[0:w, bass.ds(cc, 1), :]))
                ch.go(CP(lastP[0:w, bass.ds(cc, 1), 0:1], buf[0:w, None, 256:257]))
                ch.step(CP(lastP[0:w, bass.ds(cc, 1), 1:9], seq(buf, 257, 1, 8, 9)[0:w].rearrange("p b t -> p t b")))
                ch.step(TT(dif[0:w, :], buf[0:w, 0:328], buf[0:w, 1:329], SUB))
                m = muT[0:w, bass.ds(cc, 1)]
                ch.go(STT(out[:, 0:256], dif[0:w, 0:256], m, buf[0:w, 1:257], MUL, ADD))
                q = STT(s88(out[:, 256:N]), dif[0:w, 256:328].rearrange("p (b t) -> p b t", b=NB)[:, :, 1:9], m,
                        seq(buf, 257, 1, 1, 9)[0:w], MUL, ADD)
                if fin:
                    q.then_inc(S(fin), 1)
                else:
                    ch.step(q)

            for j, (n, w) in enumerate((("r", 128), ("k", 128), ("v", 32))):
                dve.wait_ge(S("pre_c"), j + 1)
                mix(ch, pad1[n], w, 24 + j, lw[0:w, j, :])
            for j in range(3):
                q = CP(rowst[:, 9 + j:10 + j], misc[:, 3:4])
                q.then_inc(S("mixed" if j else "pre_mix"), 1)
            CP(rowst[:, 8:9], misc[:, 3:4]).then_inc(S("mixed"), 1)
            dve.wait_ge(S("lwt"), 1)
            ch.go(TS(lw[:, 1, :], lw[:, 1, :], 0.5, 0.5, MUL, ADD))
            TS(lw[0:32, 2, :], lw[0:32, 2, :], 0.5, 0.5, MUL, ADD).then_inc(S("lw"), 1)

            def pair(i, first):
                ch = Chain(dve, S("dve_chain"), i, DVE_PER)
                go, step = ch.go, ch.step
                for j, (n, out) in enumerate((("r", rm), ("k", km), ("v", vm))):
                    taken(dve, i, n)
                    if n == "v" and not first:
                        dve.wait_ge(S("tm_ps"), i * 3)
                    mix(ch, pad1[n], P, i + 8 * j, out[:], "mixed")
                dve.wait_ge(S("mixed"), i * 3 + 6)
                step(TS(kk[:], km[:], vcol("k_k", i), None, MUL))
                TT(kk2[:], kk[:], kk[:], MUL).then_inc(S("kk2"), 1)
                taken(dve, i, "za")
                step(TS(ta[:], ta[:], 0.5, 0.5, MUL, ADD))
                step(TS(kp[:], ta[:], 1.0, vcol("k_a", i), SUB, MUL))
                step(STT(kp[:], kp[:], 1.0, km[:], ADD, MUL))
                STT(rkk[:], rm[:], vcol("r_k", i), kp[:], MUL, MUL).then_inc(S("rkk"), 1)
                dve.wait_ge(S("dec"), i + 1)
                step(TT(wsh[:, 1:N], dec[:, 0:N - 1], C("m0")[:, 1:N], MUL))
                step(nc.vector.tensor_tensor_scan(ex[:], wsh[:], C("m1"), 0.0, MUL, ADD))
                step(TT(Dc[:], ex[:], dec[:], MUL))
                step(nc.vector.reciprocal(rD[:], Dc[:]))
                tp_ready(dve, i, "ss")
                TS(nrm[:], tpbank("ss"), 1e-24, None, MAX).then_inc(S("taken_d"), 1)
                go(TT(ar[:, 1, :], rm[:], Dc[:], MUL))
                step(TT(kt[:], kp[:], rD[:], MUL))
                dve.wait_ge(S("nrm"), i + 1)
                step(nc.vector.reciprocal(nrm[:], nrm[:]))
                step(TT(kk[:], kk[:], nrm[:], MUL))
                go(STT(ar[:, 0, :], kk[:], -1.0, ex[:], MUL, MUL))
                step(TT(bt[:], kk[:], ta[:], MUL))
                TT(bt[:], bt[:], rD[:], MUL).then_inc(S("ops"), 1)
                tp_ready(dve, i, "bon")
                TT(bon[:], tpbank("bon"), vm[:], MUL).then_inc(S("taken_d"), 1)
                taken(dve, i, "lx")
                go(CP(seq(pad3, 259, 3, 0, 3), cvT[:, bass.ds(i, 1), 0:24].rearrange("p o (b j) -> p (o b) j", j=3)))
                go(CP(lastL[:, bass.ds(i, 1), 0:3], pad3[:, None, 256:259]))
                step(CP(lastL[:, bass.ds(i, 1), 3:27].rearrange("p o (b j) -> p (o b) j", j=3), seq(pad3, 259, 3, 8, 11)))
                step(TS(cacc[:, 0:344], pad3[:, 0:344], vcol("conv_w", i), vcol("conv_b", i), MUL, ADD))
                for j in (1, 2):
                    step(STT(cacc[:, 0:344], pad3[:, j:344 + j], vcol("conv_w", i, 8 * j), cacc[:, 0:344], MUL, ADD))
                go(STT(xc[:, 0:256], pad3[:, 3:259], vcol("conv_w", i, 24), cacc[:, 0:256], MUL, ADD))
                STT(s88(xc[:, 256:N]), seq(pad3, 259, 3, 3, 11), vcol("conv_w", i, 24), seq(cacc, 259, 3, 0, 8), MUL, ADD)\
                    .then_inc(S("xc"), 1)
                for u in range(4):
                    dve.wait_ge(S("big"), i * 5 + (u + 1))
                    go(TT(am[:, u, :], bank[2 + u][:], C("maskp"), MUL))
                dve.wait_ge(S("big"), i * 5 + 5)
                go(TT(ams[:, 0, :], bank[6][0:64, 0:256], C("masks")[0:64, :], MUL))
                TT(ams[:, 1, :], bank[7][0:64, 0:256], C("masks")[0:64, :], MUL).then_inc(S("am"), 1)
                dve.wait_ge(S("am"), i + 1)
                go(TT(Yp[:], am[:, :, 0:128], lev[:, 0, None, :].broadcast_to([P, 4, P]), MUL))
                step(TT(Ys[:], ams[:, :, 0:64], lev[0:64, 0, None, 0:64].broadcast_to([64, 2, 64]), MUL))
                go(TT(Yp[:], Yp[:], ident[:, None, :].broadcast_to([P, 4, P]), ADD))
                TT(Ys[:], Ys[:], ident[0:64, None, 0:64].broadcast_to([64, 2, 64]), ADD).then_inc(S("y1"), 1)
                taken(dve, i, "ly")
                step(TS(ysq[:], ysq[:], 0.044715, 1.0, MUL, ADD))
                TT(tu[:], ysq[:], ysb[:], MUL).then_inc(S("u_gelu"), 1)
                dve.wait_ge(S("akv"), i + 1)
                dve.wait_ge(S("tm"), i * 3 + 3)
                for h in range(2):
                    c = slice(64 * h, 64 * h + 64)
                    go(CP(tm[:, 0:2, 4, c], bank[5][:].rearrange("p (t h c) -> p t h c", t=2, h=2)[:, :, h, c]))
                    q = CP(tm[0:64, 2, 4, c], bank[6][0:64, 128 * h + 64 * h:128 * h + 64 * h + 64])
                    if h == 0:
                        go(q)
                q.then_inc(S("akv_c"), 1)

                def level(k):
                    dve.wait_ge(S("lvM"), i * 4 + (k + 1))
                    if k < 3:
                        go(TT(Xp[:], Xp[:], bank[3][:].rearrange("p (u t) -> p u t", u=4), ADD))
                    if k < 2:
                        go(TT(Xs[:], Xs[:], bank[6][0:64, 128:256].rearrange("p (u t) -> p u t", u=2), ADD))
                        go(TT(Ys[:], Ys[:], bank[6][0:64, 256:384].rearrange("p (u t) -> p u t", u=2), ADD))
                    TT(Yp[:], Yp[:], bank[4][:].rearrange("p (u t) -> p u t", u=4), ADD).then_inc(S("lvl"), 1)

                dve.wait_ge(S("y1"), i + 1)
                dve.wait_ge(S("x1"), i + 1)
                level(0)
                dve.wait_ge(S("la"), i + 1)
                step(TS(lm[:], lth[:], -1.0, 1.0, MUL, ADD))
                step(nc.vector.reciprocal(lm[:], lm[:]))
                step(STT(lm[:], lth[:], -2.0, lm[:], MUL, MUL))
                TS(lm[:], lm[:], 1e-34, None, MAX).then_inc(S("m2"), 1)
                level(1)
                taken(dve, i, "gx")
                step(STT(tgx[:], tgx[:], 1.0, xc[:], ADD, MUL))
                dve.wait_ge(S("tu"), i + 1)
                step(STT(tu[:], tu[:], 1.0, ysb[:], ADD, MUL))
                level(2)
                dve.wait_ge(S("lm"), i + 1)
                step(MS(lm[:, 0:1], 1.0))
                step(STT(tgx[:], tgx[:], 0.5, lm[:], MUL, MUL))
                step(TT(fix[:], la[:, 256:N:TB], cvT[:, bass.ds(i, 1), 24:32].rearrange("p o b -> p (o b)"), MUL))
                go(TT(tgx[:, 256:N:TB], tgx[:, 256:N:TB], fix[:], ADD))
                step(MS(la[:, 256:N:TB], 0.0))
                step(nc.vector.tensor_tensor_scan(hbuf[:], la[:], tgx[:], 0.0, MUL, ADD))
                level(3)
                go(CP(lastL[:, bass.ds(i, 1), 27:36], hbuf[:, None, 255:N:TB]))
                step(STT(lruo[:], tu[:], 0.25, hbuf[:], MUL, MUL))
                taken(dve, i, "gl")
                step(STT(lruo[:], tgl[:], 1.0, lruo[:], ADD, MUL))
                taken(dve, i, "gr")
                tp_ready(dve, i, "g")
                STT(gg[:], tgr[:], 1.0, tpbank("g"), ADD, MUL).then_inc(S("taken_d"), 1)
                dve.wait_ge(S("pu"), i + 1)
                for t in range(2):
                    TT(u0x[:, t], u0[:, t, None, :].broadcast_to([P, 4, P]), C("cm")[:, :, None].broadcast_to([P, 4, P]), MUL)\
                        .then_inc(S("u0x"), 1)
                dve.wait_ge(S("rh_ps"), i + 1)
                TT(rs[:, 1, :], bank[3][:, 0:N], ar[:, 1, :], ADD).then_inc(S("rhat"), 1)
                for c in range(2):
                    dve.wait_ge(S("gt_ps"), i * 2 + (c + 1))
                    TT(gt[:, 4 * c:4 * c + 4], bank[2 if c else 5][:].rearrange("p (c k) -> p c k", c=4),
                       blk[:, None, :].broadcast_to([P, 4, P]), MUL).then_inc(S("gtm"), 1)
                for c in range(NCH):
                    dve.wait_ge(S("st_ps"), i * NCH + (c + 1))
                    STT(Sst[:, c + 1, :], bank[7 if c < 4 else 3][:, 128 * (c % 4):128 * (c % 4) + 128], Dc[:, CH * c + CH - 1:CH * c + CH], blk,
                        MUL, MUL).then_inc(S("state"), 1)
                dve.wait_ge(S("y_ps"), i + 1)
                go(CP(yT[:, 0:256], bank[4][:, 0:256]))
                dve.wait_ge(S("ysm"), i + 1)
                TT(s88(yT[:, 256:N]), s88(bank[4][:, 256:N]), ysm[:, 1], ADD).then_inc(S("yT"), 1)
                dve.wait_ge(S("u_ps"), i + 1)
                dve.wait_ge(S("pu"), i + 1)
                step(TT(usb[:], bank[6][0:64, 128:256].rearrange("p (h v) -> p h v", h=2), pus[:, :, 64:128], ADD))
                for h in range(2):
                    q = TT(uex[:, h].rearrange("p (b v) -> p b v", b=NB), usb[:, h, None, :].broadcast_to([64, NB, HEAD]),
                           C("bm")[0:64, :, None].broadcast_to([64, NB, HEAD]), MUL)
                    if h == 0:
                        go(q)
                q.then_inc(S("uex"), 1)
                tp_ready(dve, i, "mean")
                dve.wait_ge(S("yT"), i + 1)
                TT(yc[:], yT[:], tpbank("mean"), SUB).then_inc(S("taken_d"), 1)
                dve.wait_ge(S("su"), i + 1)
                step(TT(s1T[:], s0T[:], bank[6][:].rearrange("p (b v) -> p b v", b=NB), ADD))
                TT(s1T[:], s1T[:], Dc[:, 256 + TB - 1:N:TB, None].broadcast_to([P, NB, 64]), MUL).then_inc(S("supd"), 1)
                taken(dve, i, "var")
                step(nc.vector.reciprocal(gns[:], gns[:]))
                step(TT(yc[:], yc[:], gns[:], MUL))
                step(TS(yc[:], yc[:], vcol("ln_w", i), vcol("ln_b", i), MUL, ADD))
                step(TT(yc[:], yc[:], bon[:], ADD))
                step(STT(yc[:], gg[:], 0.5, yc[:], MUL, MUL))
                TT(merged[:, bass.ds(i, 1), :], yc[:, None, :], lruo[:, None, :], ADD).then_inc(S("merged"), 1)
                assert ch.n == DVE_PER, ch.n

            dve.wait_ge(S("z_out"), 16 * NOV)
            pair(0, True)
            with dve.Fori(1, PAIRS) as i:
                pair(i, False)
            ch = Chain(dve, S("dve_rt"))
            go, step = ch.go, ch.step
            EQ, GE, GT, LE = ALU.is_equal, ALU.is_ge, ALU.is_gt, ALU.is_le
            RED = nc.vector.tensor_reduce
            ob = [bank[j] for j in (0, 3, 4, 6, 2, 7)]
            dve.wait_ge(S("x1_in"), 48)
            for t, (_, n) in enumerate(TILES):
                if t < 2:
                    dve.wait_ge(S("o_ps"), t + 1)
                else:
                    dve.wait_ge(S("wo_ps"), 1)
                for h in range(2):
                    c = slice(512 * h, 512 * h + 512)
                    q = TT(x1[0:n, t, c], x1[0:n, t, c], ob[2 * t + h][0:n, :], ADD)
                q.then_inc(S("x1r"), 1)
            dve.wait_ge(S("rms"), 6)
            for t, (_, n) in enumerate(TILES):
                step(nc.vector.reciprocal(rowst[0:n, 6 + t:7 + t], rowst[0:n, 3 + t:4 + t]))
                STT(xn2[0:n, t, :], x1[0:n, t, :], rowst[0:n, 6 + t:7 + t], norm2b[0:n, :], MUL, MUL).then_inc(S("xn2"), 1)
            step(MS(lg[:], 0.0))
            dve.wait_ge(S("lg_ps"), 1)
            go(CP(lg[:, 0:2, :], bank[5][:, 0:128].rearrange("p (t e) -> p t e", t=2)[:, :, 0:NG + NE]))
            step(CP(lg[0:64, 2, :], bank[5][0:64, 128:128 + NG + NE]))

            def col(j):
                return r1[:, :, j:j + 1]

            def first_max(x, m, pref, cnd, out, n):
                step(RED(col(m), x, AX.X, MAX))
                step(TT(cnd, x, col(m).broadcast_to([P, 3, n]), EQ))
                step(TT(cnd, cnd, pref[:, None, :].broadcast_to([P, 3, n]), MUL))
                step(RED(col(m + 10), cnd, AX.X, MAX))
                step(TT(out, cnd, col(m + 10).broadcast_to([P, 3, n]), EQ))

            first_max(lg[:, :, 0:NG], 0, C("g4"), cg[:], ohg[:], NG)
            TT(dg[:], lg[:, :, 0:NG], col(0).broadcast_to([P, 3, NG]), SUB).then_inc(S("dexp"), 1)
            step(TT(le[:], lg[:, :, NG:].rearrange("p t (g e) -> p t e g", g=NG), ohg[:, :, None, :].broadcast_to([P, 3, NE_G, NG]),
                    MUL))
            step(RED(leg[:], le[:], AX.X, ADD))
            first_max(leg[:], 1, C("g8"), cand[:], oh[0][:], NE_G)
            step(STT(leg[:], oh[0][:], -3e38, leg[:], MUL, ADD))
            first_max(leg[:], 2, C("g8"), cand[:], oh[1][:], NE_G)
            TT(col(6), col(2), col(1), SUB).then_inc(S("dexp"), 1)
            for q in range(2):
                go(TT(OH[q][:], ohg[:, :, :, None].broadcast_to([P, 3, NG, NE_G]),
                      oh[q][:, :, None, :].broadcast_to([P, 3, NG, NE_G]), MUL))
            ch.wait()
            TT(Mk[:], OH[0][:].rearrange("p t g e -> p t (g e)"), OH[1][:].rearrange("p t g e -> p t (g e)"), ADD).then_inc(S("Mk"), 1)
            dve.wait_ge(S("gexp"), 2)
            step(RED(col(3), dg[:], AX.X, ADD))
            step(TS(col(4), col(7), 1.0, None, ADD))
            step(TT(col(4), col(4), col(3), MUL))
            step(nc.vector.reciprocal(col(8), col(4)))
            step(TT(col(9), col(8), col(7), MUL))
            dve.wait_ge(S("cnt_ps"), 1)
            step(MS(slot[:], 0.0))
            go(CP(slot[:, 0:2, :], bank[6][:, 0:64].rearrange("p (t e) -> p t e", t=2)))
            go(CP(slot[0:64, 2, :], bank[6][0:64, 64:96]))
            step(CP(cnt[:], bank[7][:, 0:32]))
            step(TS(xe[:], cnt[:], CAP + 0.5, None, GT))
            for j in range(2, (N - 1) // CAP + 1):
                step(STT(xe[:], cnt[:], CAP * j + 0.5, xe[:], GT, ADD))
            step(nc.vector.tensor_tensor_scan(incl[:], C("ones")[:, 0:32], xe[:], 0.0, MUL, ADD))
            step(TT(exb[:], incl[:], xe[:], SUB))
            step(TS(exb[:], exb[:], float(CAP), float((NE - 1) * CAP), MUL, ADD))
            step(TT(exb[:], exb[:], C("e64"), SUB))
            OH_S = le[:].rearrange("p t e g -> p t (e g)")
            step(TS(OH_S, slot[:], CAP - 0.5, None, GT))
            step(TT(OH_S, OH_S, exb[:, None, :].broadcast_to([P, 3, NE]), MUL))
            go(TT(slot[:], slot[:], C("e64")[:, None, :].broadcast_to([P, 3, NE]), ADD))
            ch.wait()
            step(TT(slot[:], slot[:], OH_S, ADD))
            for q in range(2):
                step(TT(OH_S, OH[q][:].rearrange("p t g e -> p t (g e)"), slot[:], MUL))
                step(RED(col(20 + q), OH_S, AX.X, ADD))
                q2 = CP(slotu[:, q, :], r1[:, :, 20 + q])
                if q == 0:
                    go(q2)
            q2.then_inc(S("slotu"), 1)
            step(TT(le9, incl[0:1, None, :].broadcast_to([1, NOV, NE]), C("j9")[0:1, :, None].broadcast_to([1, NOV, NE]), LE))
            step(RED(ovf[:, 0:NOV], le9, AX.X, ADD))
            go(TS(ovf[:, 0:NOV], ovf[:, 0:NOV], NE - 1.0, None, MIN))
            step(CP(ovf[:, NOV:NOV + 1], incl[0:1, 31:32]))
            CP(ovi[:, 0:NOV + 1], ovf[:, 0:NOV + 1]).then_inc(S("ov"), 1)

            dve.wait_ge(S("idx_ps"), 1)
            CP(idx[:], bank[1][0:CAP, 0:NE + NOV]).then_inc(S("idx"), 1)
            def outputs(i, j, first):
                dve.wait_ge(S("dn"), i * 4 + (j + 1))
                if not (first and j < 2):
                    dve.wait_ge(S(f"y_out{j % 2}"), i * 64 + 32 * (j // 2))
                CP(ye[:, j % 2, :], bank[6 + j % 2][:]).then_inc(S("ye"), 1)

            def experts(i, first):
                for j in range(4):
                    dve.wait_ge(S("th"), i * 4 + (j + 1))
                    STT(th, th, 1.0, bank[2 + j % 2][:, 0:128], ADD, MUL).then_inc(S("thg"), 1)
                    dve.wait_ge(S("thg"), i * 4 + (j + 1))
                    if not (first and j == 0):
                        dve.wait_ge(S("hT_ps"), i * 4 + j)
                    STT(hh, th, 0.5, bank[2 + j % 2][:, 128:256], MUL, MUL).then_inc(S("h"), 1)
                    if j:
                        outputs(i, j - 1, first)
                    elif not first:
                        outputs(i + -1, 3, False)

            experts(0, True)
            with dve.Fori(1, NE // 4) as i:
                experts(i, False)
            outputs(NE // 4 - 1, 3, False)
            dve.wait_ge(S("ov"), 1)
            n_ov = dve.value_load(ovi[0:1, NOV:NOV + 1], min_val=0, max_val=NOV)
            with dve.If(n_ov > 0):
                with dve.Fori(0, NOV) as j:
                    dve.wait_ge(S("th"), j + (NE + 1))
                    STT(th, th, 1.0, bank[2][:, 0:128], ADD, MUL).then_inc(S("thg"), 1)
                    dve.wait_ge(S("thg"), j + (NE + 1))
                    STT(hh, th, 0.5, bank[2][:, 128:256], MUL, MUL).then_inc(S("h"), 1)
                    dve.wait_ge(S("dn"), j + (NE + 1))
                    dve.wait_ge(S("y_out0"), j * 32 + 16 * NE)
                    CP(ye[:, 0, :], bank[6][:]).then_inc(S("ye"), 1)
            CP(rowst[:, 9:10], misc[:, 3:4]).then_inc(S("fin0"), 1)
            for t, (_, n) in enumerate(TILES):
                dve.wait_ge(S(f"ya{t}"), 32)
                step(STT(x1[0:n, t, :], ya[0][0:n, t, :], r1[0:n, t, 8:9], x1[0:n, t, :], MUL, ADD))
                STT(x1[0:n, t, :], ya[1][0:n, t, :], r1[0:n, t, 9:10], x1[0:n, t, :], MUL, ADD).then_inc(S("x2r"), 1)
            dve.wait_ge(S("rms"), 9)
            dve.wait_ge(S("fn_in"), 16)
            for t, (_, n) in enumerate(TILES):
                step(nc.vector.reciprocal(rowst[0:n, 6 + t:7 + t], rowst[0:n, 3 + t:4 + t]))
                STT(x1[0:n, t, :], x1[0:n, t, :], rowst[0:n, 6 + t:7 + t], fnb[0:n, :], MUL, MUL).then_inc(S("y_fin"), 1)


_INS = ['x_prompt', 'x_sample', 'state_conv', 'state_lru', 'state_shift', 'state_wkv', 'norm1', 'w_in', 'conv_w', 'conv_b',
        'lru_wx', 'lru_bx', 'lru_wa', 'lru_ba', 'lru_a_param', 'rwkv_mu', 'rwkv_w0', 'rwkv_w2', 'rwkv_a0', 'rwkv_a2',
        'rwkv_g2', 'rwkv_k_k', 'rwkv_k_a', 'rwkv_r_k', 'rwkv_ln_w', 'rwkv_ln_b', 'w_out', 'norm2', 'router_group',
        'router_group_b', 'router_expert', 'router_expert_b', 'exp_gate', 'exp_up', 'exp_down', 'final_norm']
_OUTS = [("y_p", (1, 256, 1024)), ("y_s", (8, 8, 1024)), ("conv_p", (1, 1, 3, 1024)), ("lru_p", (1, 1, 1024)),
         ("shift_p", (1, 1, 3360)), ("wkv_p", (1, 1, 16, 64, 64)), ("conv_s", (1, 8, 3, 1024)), ("lru_s", (1, 8, 1024)),
         ("shift_s", (1, 8, 3360)), ("wkv_s", (1, 8, 16, 64, 64))]


def kernel(**inputs):
    import numpy as _np
    import concourse.bacc as _bacc
    from concourse import mybir as _mybir
    from concourse.bass_utils import run_bass_kernel_spmd as _run

    nc = _bacc.Bacc("TRN2", target_bir_lowering=False, num_devices=1)
    arrays, ins, outs = {}, {}, {}
    consts, ids = make_consts()
    given = {name: _np.ascontiguousarray(inputs[name]) for name in _INS}
    given["consts"], given["ids"] = consts, ids
    for name, x in given.items():
        arrays[f"in_{name}"] = x
        ins[name] = nc.dram_tensor(f"in_{name}", x.shape, _mybir.dt.from_np(x.dtype), kind="ExternalInput").ap()
    for name, shape in _OUTS:
        outs[name] = nc.dram_tensor(f"out_{name}", shape, _mybir.dt.float32, kind="ExternalOutput").ap()
    hawk_rwkv7_moe(nc, ins, outs)
    r = _run(nc, [arrays], core_ids=[0])
    return tuple(r.results[0][f"out_{name}"] for name, _ in _OUTS)
```
